# Optimizing a Trainium2 kernel written in Bass

```python
import jax, jax.numpy as jnp
from jax import lax
import numpy as np

D_MODEL = 1024
BATCH = 1
SEQ = 1024
DEPTH = 1
DEC_BATCH = 1
DEC_SEQ = 1024
PAST_LEN = 128

N_META = 16
GRID_W = 64
Q_BLOCK = 128
ROPE_BASE = 10000.0
NORM_EPS = 1e-6
GQA_HEADS = D_MODEL // 128
GQA_KV_HEADS = GQA_HEADS // 4
GQA_HEAD_DIM = 64
MLA_HEADS = D_MODEL // 128
MLA_NOPE_DIM = 64
MLA_ROPE_DIM = 32
MLA_V_DIM = 64
MLA_Q_RANK = 3 * D_MODEL // 8
MLA_KV_RANK = D_MODEL // 4
N_EXPERTS = 16
CAPACITY_FACTOR = 2
EXPERT_FF = D_MODEL // 2

IN_SPLIT_SIZES = (
    GQA_HEADS * GQA_HEAD_DIM,
    GQA_KV_HEADS * GQA_HEAD_DIM,
    GQA_KV_HEADS * GQA_HEAD_DIM,
    MLA_Q_RANK,
    MLA_KV_RANK,
    MLA_ROPE_DIM,
    2 * D_MODEL,
)
IN_COLS = int(sum(IN_SPLIT_SIZES))
IN_SPLIT_IDX = tuple(int(i) for i in np.cumsum(IN_SPLIT_SIZES)[:-1])

kernel_name = 'hybrid_gqa_mla_ec_encoder'

def _rmsnorm(x, g):
    xf = x.astype(jnp.float32)
    y = xf * lax.rsqrt(jnp.mean(xf * xf, axis=-1, keepdims=True) + NORM_EPS)
    return (y * g.astype(jnp.float32)).astype(x.dtype)

def _rope_1d(x, pos):
    half = x.shape[-1] // 2
    inv = ROPE_BASE ** (-jnp.arange(half, dtype=jnp.float32) / half)
    ang = pos[:, None] * inv[None, :]
    cos = jnp.cos(ang)[None, :, None, :]
    sin = jnp.sin(ang)[None, :, None, :]
    xf = x.astype(jnp.float32)
    x1, x2 = xf[..., :half], xf[..., half:]
    return jnp.concatenate([x1 * cos - x2 * sin, x2 * cos + x1 * sin], axis=-1).astype(x.dtype)

def _rope_2d(x, pos_row, pos_col):
    a = x.shape[-1] // 2
    return jnp.concatenate([_rope_1d(x[..., :a], pos_row), _rope_1d(x[..., a:], pos_col)], axis=-1)

def _sweep_query_blocks(q, attend):
    B, L = q.shape[0], q.shape[1]
    nb = -(-L // Q_BLOCK)
    pad = nb * Q_BLOCK - L
    qp = jnp.pad(q, [(0, 0), (0, pad)] + [(0, 0)] * (q.ndim - 2))
    qb = jnp.moveaxis(qp.reshape((B, nb, Q_BLOCK) + q.shape[2:]), 1, 0)
    out = lax.map(attend, qb)
    out = jnp.moveaxis(out, 0, 1).reshape(B, nb * Q_BLOCK, -1)
    return out[:, :L]

def _expert_choice_ffn(h, w_router, w_gate, w_up, w_down):
    B, L, D = h.shape
    n = B * L
    cap = (CAPACITY_FACTOR * n) // N_EXPERTS
    t = h.reshape(n, D)
    aff = jax.nn.softmax(jnp.matmul(t, w_router).astype(jnp.float32), axis=-1)
    g, idx = lax.top_k(aff.T, cap)
    xs = t[idx]
    hg = jnp.einsum('ecd,edf->ecf', xs, w_gate)
    hu = jnp.einsum('ecd,edf->ecf', xs, w_up)
    y = jnp.einsum('ecf,efd->ecd', jax.nn.silu(hg) * hu, w_down)
    y = y * g[..., None].astype(y.dtype)
    out = jnp.zeros((n, D), y.dtype).at[idx.reshape(-1)].add(y.reshape(-1, D))
    return out.reshape(B, L, D)

def _layer(h, pos_row, pos_col, attn_norm, w_in, gqa_q_norm, gqa_k_norm, mla_q_norm,
           mla_kv_norm, mla_w_uq, mla_w_ukv, w_o_gqa, w_o_mla, w_out, ffn_norm,
           w_router, w_gate, w_up, w_down):
    B, L, D = h.shape
    hn = _rmsnorm(h, attn_norm)
    proj = jnp.matmul(hn, w_in)
    q_g, k_g, v_g, c_q, c_kv, k_r, gates = jnp.split(proj, IN_SPLIT_IDX, axis=-1)

    q_g = _rope_2d(_rmsnorm(q_g.reshape(B, L, GQA_HEADS, GQA_HEAD_DIM), gqa_q_norm), pos_row, pos_col)
    k_g = _rope_2d(_rmsnorm(k_g.reshape(B, L, GQA_KV_HEADS, GQA_HEAD_DIM), gqa_k_norm), pos_row, pos_col)
    v_g = v_g.reshape(B, L, GQA_KV_HEADS, GQA_HEAD_DIM)
    rep = GQA_HEADS // GQA_KV_HEADS
    scale_g = 1.0 / float(np.sqrt(GQA_HEAD_DIM))

    def attend_gqa(qb):
        qb = qb.reshape(B, Q_BLOCK, GQA_KV_HEADS, rep, GQA_HEAD_DIM)
        s = jnp.einsum('bqgrd,bkgd->bgrqk', qb, k_g, preferred_element_type=jnp.float32) * scale_g
        p = jax.nn.softmax(s, axis=-1).astype(v_g.dtype)
        o = jnp.einsum('bgrqk,bkgd->bqgrd', p, v_g)
        return o.reshape(B, Q_BLOCK, GQA_HEADS * GQA_HEAD_DIM)

    o_g = _sweep_query_blocks(q_g, attend_gqa)

    q_m = jnp.matmul(_rmsnorm(c_q, mla_q_norm), mla_w_uq).reshape(B, L, MLA_HEADS, MLA_NOPE_DIM + MLA_ROPE_DIM)
    q_m = jnp.concatenate([q_m[..., :MLA_NOPE_DIM], _rope_2d(q_m[..., MLA_NOPE_DIM:], pos_row, pos_col)], axis=-1)
    kv = jnp.matmul(_rmsnorm(c_kv, mla_kv_norm), mla_w_ukv).reshape(B, L, MLA_HEADS, MLA_NOPE_DIM + MLA_V_DIM)
    k_nope, v_m = kv[..., :MLA_NOPE_DIM], kv[..., MLA_NOPE_DIM:]
    k_rope = _rope_2d(k_r[:, :, None, :], pos_row, pos_col)[:, :, 0, :]
    scale_m = 1.0 / float(np.sqrt(MLA_NOPE_DIM + MLA_ROPE_DIM))

    def attend_mla(qb):
        qn, qr = qb[..., :MLA_NOPE_DIM], qb[..., MLA_NOPE_DIM:]
        s = (jnp.einsum('bqhd,bkhd->bhqk', qn, k_nope, preferred_element_type=jnp.float32)
             + jnp.einsum('bqhd,bkd->bhqk', qr, k_rope, preferred_element_type=jnp.float32)) * scale_m
        p = jax.nn.softmax(s, axis=-1).astype(v_m.dtype)
        o = jnp.einsum('bhqk,bkhd->bqhd', p, v_m)
        return o.reshape(B, Q_BLOCK, MLA_HEADS * MLA_V_DIM)

    o_m = _sweep_query_blocks(q_m, attend_mla)

    g_a, g_b = jnp.split(gates, 2, axis=-1)
    mixed = (jax.nn.sigmoid(g_a) * jnp.matmul(o_g, w_o_gqa)
             + jax.nn.sigmoid(g_b) * jnp.matmul(o_m, w_o_mla))
    h = h + jnp.matmul(mixed, w_out)

    h = h + _expert_choice_ffn(_rmsnorm(h, ffn_norm), w_router, w_gate, w_up, w_down)
    return h

def _forward(x, meta_tokens, attn_norm, w_in, gqa_q_norm, gqa_k_norm, mla_q_norm, mla_kv_norm,
             mla_w_uq, mla_w_ukv, w_o_gqa, w_o_mla, w_out, ffn_norm, w_router, w_gate, w_up,
             w_down, final_norm):
    B, S, D = x.shape
    rows_n = S // GRID_W
    grid_row = jnp.repeat(jnp.arange(rows_n, dtype=jnp.float32), GRID_W)
    grid_col = jnp.tile(jnp.arange(GRID_W, dtype=jnp.float32), rows_n)
    pos_row = jnp.concatenate([jnp.full((N_META,), -1.0, jnp.float32), grid_row])
    pos_col = jnp.concatenate([jnp.arange(N_META, dtype=jnp.float32), grid_col])
    meta = jnp.broadcast_to(meta_tokens.astype(x.dtype)[None], (B, N_META, D))
    h = jnp.concatenate([meta, x], axis=1)
    for l in range(DEPTH):
        h = _layer(h, pos_row, pos_col, attn_norm[l], w_in[l], gqa_q_norm[l], gqa_k_norm[l],
                   mla_q_norm[l], mla_kv_norm[l], mla_w_uq[l], mla_w_ukv[l], w_o_gqa[l],
                   w_o_mla[l], w_out[l], ffn_norm[l], w_router[l], w_gate[l], w_up[l], w_down[l])
    h = _rmsnorm(h, final_norm)
    return h[:, N_META:]

def setup_inputs(seed: int = 0) -> dict:
    key = jax.random.key(seed)
    ks = jax.random.split(key, 24)
    f32 = jnp.float32

    def nrm(k, shape, scale):
        return jax.random.normal(k, shape, f32) * scale

    def gain(k, shape):
        return 1.0 + 0.05 * jax.random.normal(k, shape, f32)

    Dp = DEPTH
    return {
        'x_prompt': nrm(ks[0], (BATCH, SEQ, D_MODEL), 1.0),
        'x_sample': nrm(ks[1], (DEC_BATCH, DEC_SEQ, D_MODEL), 1.0),
        'meta_tokens': nrm(ks[2], (N_META, D_MODEL), 1.0),
        'attn_norm': gain(ks[3], (Dp, D_MODEL)),
        'w_in': nrm(ks[4], (Dp, D_MODEL, IN_COLS), D_MODEL ** -0.5),
        'gqa_q_norm': gain(ks[5], (Dp, GQA_HEAD_DIM)),
        'gqa_k_norm': gain(ks[6], (Dp, GQA_HEAD_DIM)),
        'mla_q_norm': gain(ks[7], (Dp, MLA_Q_RANK)),
        'mla_kv_norm': gain(ks[8], (Dp, MLA_KV_RANK)),
        'mla_w_uq': nrm(ks[9], (Dp, MLA_Q_RANK, MLA_HEADS * (MLA_NOPE_DIM + MLA_ROPE_DIM)), MLA_Q_RANK ** -0.5),
        'mla_w_ukv': nrm(ks[10], (Dp, MLA_KV_RANK, MLA_HEADS * (MLA_NOPE_DIM + MLA_V_DIM)), MLA_KV_RANK ** -0.5),
        'w_o_gqa': nrm(ks[11], (Dp, GQA_HEADS * GQA_HEAD_DIM, D_MODEL), (GQA_HEADS * GQA_HEAD_DIM) ** -0.5),
        'w_o_mla': nrm(ks[12], (Dp, MLA_HEADS * MLA_V_DIM, D_MODEL), (MLA_HEADS * MLA_V_DIM) ** -0.5),
        'w_out': nrm(ks[13], (Dp, D_MODEL, D_MODEL), D_MODEL ** -0.5),
        'ffn_norm': gain(ks[14], (Dp, D_MODEL)),
        'w_router': nrm(ks[15], (Dp, D_MODEL, N_EXPERTS), D_MODEL ** -0.5),
        'w_gate': nrm(ks[16], (Dp, N_EXPERTS, D_MODEL, EXPERT_FF), D_MODEL ** -0.5),
        'w_up': nrm(ks[17], (Dp, N_EXPERTS, D_MODEL, EXPERT_FF), D_MODEL ** -0.5),
        'w_down': nrm(ks[18], (Dp, N_EXPERTS, EXPERT_FF, D_MODEL), EXPERT_FF ** -0.5),
        'final_norm': gain(ks[19], (D_MODEL,)),
    }

def reference(x_prompt, x_sample, meta_tokens, attn_norm, w_in, gqa_q_norm, gqa_k_norm,
              mla_q_norm, mla_kv_norm, mla_w_uq, mla_w_ukv, w_o_gqa, w_o_mla, w_out,
              ffn_norm, w_router, w_gate, w_up, w_down, final_norm):
    y_prompt = _forward(x_prompt, meta_tokens, attn_norm, w_in, gqa_q_norm, gqa_k_norm,
                        mla_q_norm, mla_kv_norm, mla_w_uq, mla_w_ukv, w_o_gqa, w_o_mla,
                        w_out, ffn_norm, w_router, w_gate, w_up, w_down, final_norm)
    y_sample = _forward(x_sample, meta_tokens, attn_norm, w_in, gqa_q_norm, gqa_k_norm,
                        mla_q_norm, mla_kv_norm, mla_w_uq, mla_w_ukv, w_o_gqa, w_o_mla,
                        w_out, ffn_norm, w_router, w_gate, w_up, w_down, final_norm)
    return (y_prompt, y_sample)


_drawn_inputs = setup_inputs


def setup_inputs(seed=0):
    import zlib

    import numpy as np

    out = dict(_drawn_inputs(seed))
    spreads = {}
    factors = {'meta_tokens': 5.247,
     'attn_norm': 6.429,
     'gqa_q_norm': 8.0,
     'gqa_k_norm': 8.0,
     'mla_q_norm': 8.0,
     'mla_kv_norm': 6.921,
     'ffn_norm': 8.0}
    for name, (base, spread) in spreads.items():
        noise = np.random.default_rng([zlib.crc32(name.encode()), seed]).standard_normal(out[name].shape)
        drawn = base * np.exp(spread * noise) if base else spread * noise
        out[name] = __import__('jax').numpy.asarray(drawn.astype(out[name].dtype))
    for name, factor in factors.items():
        out[name] = (out[name] * factor).astype(out[name].dtype)
    return out
```

```python
from contextlib import ExitStack

import concourse.bass as bass
from concourse import mybir

F32 = mybir.dt.float32
F32R = mybir.dt.float32r
I32 = mybir.dt.int32
U32 = mybir.dt.uint32
ALU = mybir.AluOpType
ACT = mybir.ActivationFunctionType
AX_X = mybir.AxisListType.X

P = 128
D = 1024
DK = D // P
GROUPS = 2
SEQ = 1024
META = 16
TOK = SEQ + META
XCH = SEQ // P
STEPS = GROUPS * XCH + 1
EPS = 1e-6
HEADS = 8
KV = 2
HD = 64
NOPE = 64
ROT = 32
QK_M = NOPE + ROT
VD = 64
QR = 384
KVR = 256
QRK = QR // P
KVRK = KVR // P
Q0, K0, V0, CQ0, CKV0, KR0 = 0, 512, 640, 768, 1152, 1408
TOKEN_COLS = KR0 + ROT
E = 16
FF = 512
CAP = 2 * TOK // E
MAGIC = 0x5F3759DF
NEWTON = 3
RSQRT_OPS = 3 + 3 * NEWTON
HALF_CAP = CAP // 2
FK = FF // P
SLABS = FK + 2
SLAB = 2 * DK * P
RAW = 3


def rows_of(s):
    return META if isinstance(s, int) and s == STEPS - 1 else P


class Chain:

    def __init__(self, eng, sem, per_step, s):
        self.eng, self.sem, self.per_step, self.s, self.n = eng, sem, per_step, s, 0

    def __call__(self, ins):
        self.n += 1
        ins.then_inc(self.sem, 1)
        self.eng.wait_ge(self.sem, self.s * self.per_step + self.n)

    def end(self):
        assert self.n == self.per_step, (self.n, self.per_step)


def rsqrt(dve, link, v, mean, y, a):
    link(dve.tensor_scalar(v, mean, EPS, None, ALU.add))
    link(dve.tensor_scalar(y.bitcast(I32), v.bitcast(I32), 1, None, ALU.logical_shift_right))
    link(dve.tensor_scalar(y.bitcast(I32), y.bitcast(I32), -1.0, float(MAGIC), ALU.mult, ALU.add))
    for _ in range(NEWTON):
        link(dve.tensor_tensor(a, y, y, ALU.mult))
        link(dve.scalar_tensor_tensor(a, a, -0.5, v, ALU.mult, ALU.mult))
        link(dve.scalar_tensor_tensor(y, a, 1.5, y, ALU.add, ALU.mult))


def spread(ap, axis, n):
    shape = list(ap.shape)
    shape.insert(axis, n)
    return ap.unsqueeze(axis).broadcast_to(tuple(shape))


def identity_matrix(pool, ident, ident_ready):
    pool.memset(ident[:, :], 0.0).then_inc(ident_ready, 1)
    pool.wait_ge(ident_ready, 1)
    pool.affine_select(out=ident[:, :], in_=ident[:, :], compare_op=ALU.not_equal, fill=1.0, base=0,
                       pattern=[[-1, P]], channel_multiplier=1).then_inc(ident_ready, 1)


def scratch_tensors(nc):
    def t(name, shape):
        return nc.dram_tensor(name, shape, F32).ap()
    return dict(
        hn_t=t("hn_t", [2, GROUPS, P, DK, TOK]),
        lat_t=t("lat_t", [2, GROUPS, P, QRK + KVRK, TOK]),
        k_rot=t("k_rot", [GROUPS, TOK, ROT]),
        gq_t=t("gq_t", [GROUPS, HEADS, P, TOK]),
        gk_t=t("gk_t", [2, GROUPS, KV, P, TOK]),
        gv=t("gv", [GROUPS, TOK, KV, 2 * HD]),
        mq_t=t("mq_t", [2, GROUPS, HEADS, QK_M, TOK]),
        mk_t=t("mk_t", [2, GROUPS, HEADS, QK_M, TOK]),
        mv=t("mv", [GROUPS, TOK, HEADS, 2 * VD]),
        o_t=t("o_t", [2, 2, GROUPS, HEADS * HD, TOK]),
        mix_t=t("mix_t", [2, GROUPS, P, DK, TOK]),
        h_rows=t("h_rows", [GROUPS * TOK, D]),
        t_rows=t("t_rows", [GROUPS * TOK, D]),
        aff_t=t("aff_t", [GROUPS * E, TOK]),
    )


def load_slab(sp, io, raw, e, j, loaded):
    one = bass.ds(e, 1)
    if j < FK:
        dst = raw[:, j % RAW, :].rearrange("p (a k n) -> p a k n", a=2, k=DK)
        for a, name in enumerate(("w_gate", "w_up")):
            sp.dma_start(dst[:, a, :, :], io[name][0, one, :, j * P:(j + 1) * P]
                         .rearrange("o (k p) n -> p (o k) n", p=P)).then_inc(loaded[j % RAW], 16)
    else:
        dst = raw[:, j % RAW, :].rearrange("p (k n) -> p k n", k=FK)
        half = (j - FK) * 512
        src = io["w_down"][0, one, :, half:half + 512].rearrange("o (k p) n -> p (o k) n", p=P)
        for a in range(2):
            sp.dma_start(dst[:, 2 * a:2 * a + 2, :], src[:, 2 * a:2 * a + 2, :]).then_inc(loaded[j % RAW], 16)


def valid(s):
    return not isinstance(s, int) or 0 <= s < STEPS


def at_least(eng, semaphore, value):
    if not isinstance(value, int) or value > 0:
        eng.wait_ge(semaphore, value)


def wait_alone(eng, semaphore, value, passed):
    if not isinstance(value, int) or value > 0:
        eng.wait_ge(semaphore, value)
        eng.sem_inc(passed, 1)


def tile_index(s, g):
    return s // 2 if isinstance(s, int) else (s - g) // 2


def place(s, g):
    if isinstance(s, int) and s == STEPS - 1:
        return range(GROUPS), slice(SEQ, TOK)
    return [g], bass.ds(tile_index(s, g) * P, P)


def steps(eng, body, before, after):
    first, last = (after + 3) // 2 * 2, (STEPS - 1 - before) // 2 * 2
    for j in range(-before, first):
        body(j, j % 2)
    with eng.Fori(first // 2, last // 2) as i:
        for parity in range(2):
            body(2 * i + parity, parity)
    for j in range(last, STEPS + after):
        body(j, j % 2)


class Fills:

    def __init__(self, kinds, before, after):
        order = [(kind, j + off) for j in range(-before, STEPS + after) for kind, off in kinds
                 if 0 <= j + off < STEPS]
        self.number = {key: n for n, key in enumerate(order)}
        self.per_step = len(kinds)

    def __call__(self, kind, s, g):
        if isinstance(s, int):
            n = self.number[kind, s]
            return n, n % 2
        ref = 4 + g
        n = self.number[kind, ref]
        return self.per_step * (s - ref) + n, n % 2


def rope_halves(t):
    v = t.rearrange("p h (a b c) -> p h a b c", a=2, b=2)
    return v[:, :, :, 0, :], v[:, :, :, 1, :]


def split_product(pe, out_of, k_tiles, hi_of, lo_of, w_hi, w_lo, spans, k_ready=None, between=None):
    for k in range(k_tiles):
        if k_ready:
            k_ready(k)
        for n, (left, right) in enumerate(((hi_of(k), w_hi), (hi_of(k), w_lo), (lo_of(k), w_hi))):
            for c, (lo, hi) in enumerate(spans):
                ins = pe.matmul(out_of(c, hi - lo), left, right[:, k, lo:hi],
                                start=(k == 0 and n == 0), stop=(k == k_tiles - 1 and n == 2))
        if between:
            between(k)
    return ins


def project(nc, io, scr):
    N = STEPS
    STAGED = 4
    with ExitStack() as ctx:
        def sb(name, shape, dt=F32):
            return ctx.enter_context(nc.sbuf_tensor("a_" + name, shape, dt))

        def sem(name):
            return nc.alloc_semaphore("a_" + name)

        raw = sb("raw", [P, STAGED, TOKEN_COLS])
        w_hi, w_lo = sb("w_hi", [P, DK, TOKEN_COLS], F32R), sb("w_lo", [P, DK, TOKEN_COLS], F32R)
        attn_gain, q_gain, kv_gain = sb("attn_gain", [P, D]), sb("q_gain", [P, QR]), sb("kv_gain", [P, KVR])
        head_gain = sb("head_gain", [P, HEADS + KV, HD])
        table, meta_table = sb("table", [P, XCH, 192]), sb("meta_table", [META, 192])
        ident = sb("ident", [P, P])
        x = sb("x", [P, 2, D])
        unused, unused_latent = sb("unused", [P, D]), sb("unused_latent", [P, QR + KVR])
        square = sb("square", [P, HEADS + KV, HD])
        normed, turn_sin = sb("normed", [P, HEADS + KV, HD]), sb("turn_sin", [P, HEADS + KV, HD])
        hn = sb("hn", [P, D])
        hn_hi, hn_lo = sb("hn_hi", [P, 2, DK, P], F32R), sb("hn_lo", [P, 2, DK, P], F32R)
        proj = sb("proj", [P, 2, TOKEN_COLS])
        turned = sb("turned", [P, HEADS + KV, 2, HD])
        q_st = sb("q_st", [P, HEADS, P], F32R)
        kc_hi, kc_lo = sb("kc_hi", [P, KV + QRK + KVRK, P], F32R), sb("kc_lo", [P, KV + QRK + KVRK, P], F32R)
        latent = sb("latent", [P, QR + KVR])
        v_st = sb("v_st", [P, KV, 2 * HD], F32R)
        k_rot, rot_a, rot_b = sb("k_rot", [P, 2, ROT]), sb("rot_a", [P, 1, ROT]), sb("rot_b", [P, 1, ROT])
        mean, rs = sb("mean", [P, 13]), sb("rs", [P, 3, 13])
        acc = ctx.enter_context(nc.psum_tensor("a_acc", [P, 3, 512], F32))
        tp = ctx.enter_context(nc.psum_tensor("a_tp", [P, 2, 8, P], F32))
        acc_flat = acc[:, :, :].rearrange("p a b -> p (a b)")

        x_loaded = [sem("x_loaded0"), sem("x_loaded1")]
        gain_loaded, const_loaded, sp_passed = sem("gain_loaded"), sem("const_loaded"), sem("sp_passed")
        piece_loaded = [sem(f"piece_loaded{k}") for k in range(STAGED)]
        piece_hi, piece_lo = sem("piece_hi"), sem("piece_lo")
        ident_ready = sem("ident_ready")
        x_squared, hn_ready, hn_chain = sem("x_squared"), sem("hn_ready"), sem("hn_chain")
        tp_filled, tp_hi, tp_lo = sem("tp_filled"), sem("tp_hi"), sem("tp_lo")
        proj_filled, proj_act, proj_dve = sem("proj_filled"), sem("proj_act"), sem("proj_dve")
        heads_squared, post_chain, post_done = sem("heads_squared"), sem("post_chain"), sem("post_done")
        v_hi, v_split, pool_passed = sem("v_hi"), sem("v_split"), sem("pool_passed")
        hn_stored = [sem("hn_stored0"), sem("hn_stored1")]
        qkv_stored = sem("qkv_stored")
        block = ctx.enter_context(nc.Block())

        fill = Fills((("hnT", 1), ("qT", -1), ("kcT", -1)), 1, 1)
        STORES = 16 * 7
        CONSTS = 16 * (4 + HEADS + KV)
        HALF = 1024

        def table_of(s, g, lo, hi, r):
            if isinstance(s, int) and s == N - 1:
                return meta_table[:, lo:hi]
            return table[:, bass.ds(tile_index(s, g), 1), lo:hi].rearrange("p o c -> p (o c)")

        @block.sync
        def _(sp):
            def load_x(s, g):
                wait_alone(sp, hn_ready, s - 1, sp_passed)
                if isinstance(s, int) and s == N - 1:
                    sp.dma_start(x[0:META, g, :], io["meta_tokens"]).then_inc(x_loaded[g], 16)
                else:
                    sp.dma_start(x[:, g, :], io["x_prompt" if g == 0 else "x_sample"][0, bass.ds(tile_index(s, g) * P, P), :])\
                        .then_inc(x_loaded[g], 16)

            load_x(0, 0)
            sp.dma_start(attn_gain[:, :], spread(io["attn_norm"][0, :], 0, P)).then_inc(gain_loaded, 16)
            for k in range(DK):
                at_least(sp, piece_lo, k - STAGED + 1)
                sp.dma_start(raw[:, k % STAGED, :], io["w_in"][0, k * P:(k + 1) * P, 0:TOKEN_COLS])\
                    .then_inc(piece_loaded[k % STAGED], 16)
                if k == DK // 2:
                    load_x(1, 1)
                    sp.dma_start(q_gain[:, :], spread(io["mla_q_norm"][0, :], 0, P)).then_inc(const_loaded, 16)
                    sp.dma_start(kv_gain[:, :], spread(io["mla_kv_norm"][0, :], 0, P)).then_inc(const_loaded, 16)
                    sp.dma_start(table[:, :, :], io["rope"][0:SEQ, :].rearrange("(i p) c -> p i c", p=P))\
                        .then_inc(const_loaded, 16)
                    sp.dma_start(meta_table[:, :], io["rope"][SEQ:TOK, :]).then_inc(const_loaded, 16)
                    for h in range(HEADS + KV):
                        gain = io["gqa_q_norm" if h < HEADS else "gqa_k_norm"][0, :]
                        sp.dma_start(head_gain[:, h, :], spread(gain, 0, P)).then_inc(const_loaded, 16)

            def body(j, parity):
                s, g = j + 2, parity
                if valid(s) and not (isinstance(s, int) and s < 2):
                    load_x(s, g)
                s, g = j + 1, 1 - parity
                if valid(s):
                    groups, cols = place(s, g)
                    r = rows_of(s)
                    wait_alone(sp, tp_lo, fill("hnT", s, g)[0] + 1, sp_passed)
                    for gg in groups:
                        for part, tile in enumerate((hn_hi, hn_lo)):
                            sp.dma_start(scr["hn_t"][part, gg, :, :, cols], tile[:, g, :, 0:r].bitcast(F32))\
                                .then_inc(hn_stored[g], 16)
                s, g = j - 1, 1 - parity
                if valid(s):
                    groups, cols = place(s, g)
                    r = rows_of(s)
                    wait_alone(sp, tp_lo, fill("kcT", s, g)[0] + 1, sp_passed)
                    wait_alone(sp, v_split, s + 1, sp_passed)
                    wait_alone(sp, post_done, s + 1, sp_passed)
                    for gg in groups:
                        sp.dma_start(scr["gq_t"][gg, :, :, cols].rearrange("h p n -> p h n"),
                                     q_st[:, :, 0:r].bitcast(F32)).then_inc(qkv_stored, 16)
                        for part, tile in enumerate((kc_hi, kc_lo)):
                            sp.dma_start(scr["gk_t"][part, gg, :, :, cols].rearrange("h p n -> p h n"),
                                         tile[:, 0:KV, 0:r].bitcast(F32)).then_inc(qkv_stored, 16)
                            sp.dma_start(scr["lat_t"][part, gg, :, :, cols], tile[:, KV:, 0:r].bitcast(F32))\
                                .then_inc(qkv_stored, 16)
                        sp.dma_start(scr["gv"][gg, cols, :, :], v_st[0:r, :, :].bitcast(F32)).then_inc(qkv_stored, 16)
                        sp.dma_start(scr["k_rot"][gg, cols, :], k_rot[0:r, g, :]).then_inc(qkv_stored, 16)

            steps(sp, body, 1, 1)
            sp.wait_ge(qkv_stored, STORES * (N + 1))
            sp.wait_ge(hn_stored[0], 32 * ((N + 1) // 2 + 1))
            sp.wait_ge(hn_stored[1], 32 * (N // 2))

        @block.tensor
        def _(pe):
            def turn(kind, s, g, tiles):
                n, b = fill(kind, s, g)
                r = rows_of(s)
                at_least(pe, tp_hi, n - 1)
                at_least(pe, tp_lo, n - 1)
                for k, tile in enumerate(tiles):
                    ins = pe.transpose(tp[:, b, k, 0:r], tile, ident[0:r, 0:r])
                ins.then_inc(tp_filled, 1)

            pe.wait_ge(ident_ready, 2)

            def turn_input(s, g):
                if valid(s):
                    r = rows_of(s)
                    pe.wait_ge(hn_ready, s + 1)
                    turn("hnT", s, g, [hn[0:r, k * P:(k + 1) * P] for k in range(DK)])

            def body(j, parity):
                s, g = j, parity
                if valid(s):
                    r = rows_of(s)
                    pe.wait_ge(tp_lo, fill("hnT", s, g)[0] + 1)
                    at_least(pe, proj_act, s)
                    at_least(pe, proj_dve, s)

                    def piece_ready(k):
                        pe.wait_ge(piece_lo, k + 1)

                    def between(k):
                        if k == DK // 2:
                            turn_input(j + 1, 1 - parity)
                    split_product(pe, lambda c, w: acc[0:r, c, 0:w], DK, lambda k: hn_hi[:, g, k, 0:r],
                                  lambda k: hn_lo[:, g, k, 0:r], w_hi, w_lo,
                                  [(0, 512), (512, 1024), (1024, TOKEN_COLS)],
                                  piece_ready if isinstance(s, int) and s == 0 else None, between)\
                        .then_inc(proj_filled, 1)
                else:
                    turn_input(j + 1, 1 - parity)
                s, g = j - 1, 1 - parity
                if valid(s):
                    r = rows_of(s)
                    pe.wait_ge(post_done, s + 1)
                    turn("qT", s, g, [turned[0:r, h, :, :].rearrange("p a b -> p (a b)") for h in range(HEADS)])
                    turn("kcT", s, g,
                         [turned[0:r, HEADS + h, :, :].rearrange("p a b -> p (a b)") for h in range(KV)]
                         + [latent[0:r, k * P:(k + 1) * P] for k in range(QRK + KVRK)])
            steps(pe, body, 1, 1)

        @block.scalar
        def _(act):
            def copy_hi(kind, s, g, out_of, n_tiles):
                n, b = fill(kind, s, g)
                r = rows_of(s)
                act.wait_ge(tp_filled, n + 1)
                act.copy(out_of(r), tp[:, b, 0:n_tiles, 0:r]).then_inc(tp_hi, 1)

            def body(j, parity):
                s, g = j + 1, 1 - parity
                if valid(s):
                    r = rows_of(s)
                    act.wait_ge(x_loaded[g], 16 * tile_index(s, g) + 16)
                    at_least(act, hn_ready, s)
                    act.activation(unused[0:r, :], x[0:r, g, :], ACT.Square, scale=D ** -0.5,
                                   accum_out=mean[0:r, 12:13]).then_inc(x_squared, 1)
                s, g = j - 1, 1 - parity
                if valid(s):
                    r = rows_of(s)
                    act.wait_ge(proj_act, s + 1)
                    act.wait_ge(proj_dve, s + 1)
                    at_least(act, post_done, s)
                    t = proj[0:r, g, :]
                    act.activation(square[0:r, :, :].rearrange("p h d -> p (h d)"), t[:, Q0:V0], ACT.Square,
                                   scale=HD ** -0.5).then_inc(heads_squared, 1)
                    act.activation(unused_latent[0:r, 0:QR], t[:, CQ0:CKV0], ACT.Square, scale=QR ** -0.5,
                                   accum_out=mean[0:r, 10:11]).then_inc(heads_squared, 1)
                    act.activation(unused_latent[0:r, QR:QR + KVR], t[:, CKV0:KR0], ACT.Square, scale=KVR ** -0.5,
                                   accum_out=mean[0:r, 11:12]).then_inc(heads_squared, 1)
                if isinstance(j, int) and j == -1:
                    for k in range(DK):
                        act.wait_ge(piece_loaded[k % STAGED], 16 * (k // STAGED + 1))
                        act.copy(w_hi[:, k, :], raw[:, k % STAGED, :]).then_inc(piece_hi, 1)
                        if k == 1:
                            copy_hi("hnT", 0, 0, lambda r: hn_hi[:, 0, :, 0:r], DK)
                s, g = j + 1, 1 - parity
                if valid(s) and not (isinstance(j, int) and j == -1):
                    at_least(act, hn_stored[g], 32 * tile_index(s, g))
                    copy_hi("hnT", s, g, lambda r: hn_hi[:, g, :, 0:r], DK)
                s, g = j, parity
                if valid(s):
                    r = rows_of(s)
                    act.wait_ge(proj_filled, s + 1)
                    at_least(act, v_split, s - 1)
                    at_least(act, post_done, s - 1)
                    act.copy(proj[0:r, g, 0:HALF], acc_flat[0:r, 0:HALF]).then_inc(proj_act, 1)
                s, g = j - 1, 1 - parity
                if valid(s):
                    at_least(act, qkv_stored, STORES * s)
                    copy_hi("qT", s, g, lambda r: q_st[:, :, 0:r], HEADS)
                    copy_hi("kcT", s, g, lambda r: kc_hi[:, :, 0:r], KV + QRK + KVRK)

            steps(act, body, 1, 1)

        POST_LINKS = 1 + RSQRT_OPS + 2 + 3

        @block.vector
        def _(dve):
            def split_lo(kind, s, g, out_of, hi_of, n_tiles, parts):
                n, b = fill(kind, s, g)
                r = rows_of(s)
                dve.wait_ge(tp_hi, n + 1)
                dve.tensor_tensor(out_of(r), tp[parts, b, 0:n_tiles, 0:r], hi_of(r).bitcast(F32), ALU.subtract)\
                    .then_inc(tp_lo, 1)

            def body(j, parity):
                has_input, has_heads = valid(j + 1), valid(j - 1)
                if has_heads:
                    r = rows_of(j - 1)
                    link = Chain(dve, post_chain, POST_LINKS, j - 1)
                    if isinstance(j, int) and j == 1:
                        dve.wait_ge(const_loaded, CONSTS)
                    dve.wait_ge(heads_squared, 3 * (j - 1) + 3)
                    link(dve.tensor_reduce(mean[0:r, 0:10], square[0:r, :, :], AX_X, ALU.add))
                else:
                    r = rows_of(j + 1)
                    link = Chain(dve, hn_chain, RSQRT_OPS, j + 1)
                if has_input:
                    dve.wait_ge(x_squared, j + 2)
                cols = slice(0 if has_heads else 12, 13 if has_input else 12)
                rsqrt(dve, link, rs[0:r, 0, cols], mean[0:r, cols], rs[0:r, 1, cols], rs[0:r, 2, cols])
                s, g = j + 1, 1 - parity
                if has_input:
                    r = rows_of(s)
                    if isinstance(s, int) and s == 0:
                        dve.wait_ge(gain_loaded, 16)
                    if not (isinstance(s, int) and s == 0):
                        dve.wait_ge(tp_filled, fill("hnT", s - 1, 1 - g)[0] + 1)
                    dve.scalar_tensor_tensor(hn[0:r, :], x[0:r, g, :], rs[0:r, 1, 12:13], attn_gain[0:r, :],
                                             ALU.mult, ALU.mult).then_inc(hn_ready, 1)
                if not has_heads:
                    link.end()
                s, g = j - 1, 1 - parity
                if valid(s):
                    r = rows_of(s)
                    t = proj[0:r, g, :]
                    y = rs[0:r, 1, :]
                    at_least(dve, qkv_stored, STORES * (s - 1))
                    if not (isinstance(s, int) and s == 0):
                        dve.wait_ge(tp_filled, fill("kcT", s - 1, 1 - g)[0] + 1)
                    heads = t[:, Q0:V0].rearrange("p (h d) -> p h d", d=HD)
                    nr, sn = normed[0:r, :, :], turn_sin[0:r, :, :]
                    link(dve.tensor_tensor(nr, heads, spread(y[:, 0:10], 2, HD), ALU.mult))
                    link(dve.tensor_tensor(nr, nr, head_gain[0:r, :, :], ALU.mult))
                    cos, sin = table_of(s, g, 0, 64, r), table_of(s, g, 64, 128, r)
                    cos_r, sin_r = table_of(s, g, 128, 160, r), table_of(s, g, 160, 192, r)
                    (b0, b1), (n0, n1) = rope_halves(sn), rope_halves(nr)
                    s0, s1 = rope_halves(spread(sin, 1, 10))
                    kr, ra, rb = t[:, KR0:KR0 + ROT].unsqueeze(1), rot_a[0:r, :, :], rot_b[0:r, :, :]
                    (rb0, rb1), (r0, r1), (rs0, rs1) = rope_halves(rb), rope_halves(kr), rope_halves(sin_r.unsqueeze(1))
                    dve.tensor_tensor(b0, n1, s0, ALU.mult)
                    dve.tensor_tensor(ra, kr, cos_r.unsqueeze(1), ALU.mult)
                    dve.tensor_tensor(rb0, r1, rs0, ALU.mult)
                    link(dve.tensor_tensor(b1, n0, s1, ALU.mult))
                    link(dve.tensor_tensor(nr, nr, spread(cos, 1, 10), ALU.mult))
                    link(dve.tensor_tensor(rb1, r0, rs1, ALU.mult))
                    dve.tensor_tensor(turned[0:r, :, :, :], spread(nr, 2, 2), spread(sn, 2, 2), ALU.add)
                    dve.tensor_tensor(k_rot[0:r, g:g + 1, :], ra, rb, ALU.add)
                    dve.scalar_tensor_tensor(latent[0:r, 0:QR], t[:, CQ0:CKV0], y[:, 10:11], q_gain[0:r, :],
                                             ALU.mult, ALU.mult)
                    dve.scalar_tensor_tensor(latent[0:r, QR:QR + KVR], t[:, CKV0:KR0], y[:, 11:12],
                                             kv_gain[0:r, :], ALU.mult, ALU.mult).then_inc(post_done, 1)
                    link.end()
                if isinstance(j, int) and j == -1:
                    for k in range(DK):
                        dve.wait_ge(piece_hi, k + 1)
                        dve.tensor_tensor(w_lo[:, k, :], raw[:, k % STAGED, :], w_hi[:, k, :].bitcast(F32), ALU.subtract)\
                            .then_inc(piece_lo, 1)
                        if k == 1:
                            split_lo("hnT", 0, 0, lambda r: hn_lo[:, 0, :, 0:r], lambda r: hn_hi[:, 0, :, 0:r], DK,
                                     slice(0, P))
                s, g = j + 1, 1 - parity
                if valid(s) and not (isinstance(j, int) and j == -1):
                    split_lo("hnT", s, g, lambda r: hn_lo[:, g, :, 0:r], lambda r: hn_hi[:, g, :, 0:r], DK,
                             slice(0, P))
                s, g = j, parity
                if valid(s):
                    r = rows_of(s)
                    dve.wait_ge(proj_filled, s + 1)
                    at_least(dve, v_split, s - 1)
                    dve.tensor_copy(proj[0:r, g, HALF:], acc_flat[0:r, HALF:TOKEN_COLS]).then_inc(proj_dve, 1)
                s, g = j - 1, 1 - parity
                if valid(s):
                    split_lo("qT", s, g, lambda r: q_st[HD:P, :, 0:r], lambda r: q_st[HD:P, :, 0:r], HEADS,
                             slice(HD, P))
                    split_lo("kcT", s, g, lambda r: kc_lo[:, :, 0:r], lambda r: kc_hi[:, :, 0:r],
                             KV + QRK + KVRK, slice(0, P))

            steps(dve, body, 1, 1)

        @block.gpsimd
        def _(pool):
            identity_matrix(pool, ident, ident_ready)

            def body(j, parity):
                s, g = j - 1, 1 - parity
                if valid(s):
                    r = rows_of(s)
                    pool.wait_ge(proj_act, s + 1)
                    pool.wait_ge(proj_dve, s + 1)
                    at_least(pool, qkv_stored, STORES * s)
                    v = proj[0:r, g, V0:CQ0].rearrange("p (h d) -> p h d", d=HD)
                    pool.sem_inc(pool_passed, 1)
                    pool.tensor_copy(v_st[0:r, :, 0:HD], v).then_inc(v_hi, 1)
                    pool.wait_ge(v_hi, s + 1)
                    pool.tensor_tensor(v_st[0:r, :, HD:], v, v_st[0:r, :, 0:HD].bitcast(F32), ALU.subtract)\
                        .then_inc(v_split, 1)

            steps(pool, body, 1, 1)


def latents(nc, io, scr):
    N = STEPS
    with ExitStack() as ctx:
        def sb(name, shape, dt=F32):
            return ctx.enter_context(nc.sbuf_tensor("l_" + name, shape, dt))

        def sem(name):
            return nc.alloc_semaphore("l_" + name)

        raw_uq, raw_ukv = sb("raw_uq", [P, QRK, HEADS * QK_M]), sb("raw_ukv", [P, KVRK, D])
        uq_hi, uq_lo = sb("uq_hi", [P, QRK, HEADS * QK_M], F32R), sb("uq_lo", [P, QRK, HEADS * QK_M], F32R)
        ukv_hi, ukv_lo = sb("ukv_hi", [P, KVRK, D], F32R), sb("ukv_lo", [P, KVRK, D], F32R)
        table, meta_table = sb("table", [P, XCH, 64]), sb("meta_table", [META, 64])
        ident = sb("ident", [P, P])
        lat = sb("lat", [P, 2, 2, QRK + KVRK, P], F32R)
        k_rot = sb("k_rot", [P, 2, ROT])
        qm, km = sb("qm", [P, 2, HEADS, QK_M]), sb("km", [P, 2, HEADS, QK_M])
        vm_st = sb("vm_st", [P, 2, HEADS, 2 * VD], F32R)
        rot_a, rot_b = sb("rot_a", [P, HEADS, ROT]), sb("rot_b", [P, HEADS, ROT])
        m_hi, m_lo = sb("m_hi", [QK_M, 2, 2, HEADS, P], F32R), sb("m_lo", [QK_M, 2, 2, HEADS, P], F32R)
        acc = ctx.enter_context(nc.psum_tensor("l_acc", [P, 4, 512], F32))
        tp = ctx.enter_context(nc.psum_tensor("l_tp", [P, 2, 8, P], F32))
        kv_acc = acc[:, 2:4, :].rearrange("p a b -> p (a b)").rearrange("p (h d) -> p h d", d=NOPE + VD)

        piece_loaded, table_loaded = [sem(f"piece_loaded{k}") for k in range(QRK + KVRK)], sem("table_loaded")
        piece_hi, piece_lo = sem("piece_hi"), sem("piece_lo")
        pieces = ([("mla_w_uq", k, raw_uq, uq_hi, uq_lo) for k in range(QRK)]
                  + [("mla_w_ukv", k, raw_ukv, ukv_hi, ukv_lo) for k in range(KVRK)])
        ident_ready, sp_passed, pool_passed = sem("ident_ready"), sem("sp_passed"), sem("pool_passed")
        loaded, k_rot_loaded = [sem("loaded0"), sem("loaded1")], [sem("k_rot_loaded0"), sem("k_rot_loaded1")]
        up_filled, up_act, up_dve = sem("up_filled"), sem("up_act"), sem("up_dve")
        tp_filled, tp_hi, tp_lo = sem("tp_filled"), sem("tp_hi"), sem("tp_lo")
        rope_chain, rope_done, km_done = sem("rope_chain"), sem("rope_done"), sem("km_done")
        stored, mv_stored = [sem("stored0"), sem("stored1")], [sem("mv_stored0"), sem("mv_stored1")]
        block = ctx.enter_context(nc.Block())
        fill = Fills((("mqT", -1), ("mkT", -1)), 1, 1)
        LOADS, STORES = 16 * 2, 16 * 4

        @block.sync
        def _(sp):
            def load(s, g):
                groups, cols = place(s, g)
                gg, r = groups[0], rows_of(s)
                wait_alone(sp, up_filled, s - 1, sp_passed)
                for part in range(2):
                    sp.dma_start(lat[:, g, part, :, 0:r].bitcast(F32), scr["lat_t"][part, gg, :, :, cols])\
                        .then_inc(loaded[g], 16)
                wait_alone(sp, km_done, s - 1, sp_passed)
                sp.dma_start(k_rot[0:r, g, :], scr["k_rot"][gg, cols, :]).then_inc(k_rot_loaded[g], 16)

            load(0, 0)
            for n, (name, k, raw, _, _) in enumerate(pieces):
                sp.dma_start(raw[:, k, :], io[name][0, k * P:(k + 1) * P, :]).then_inc(piece_loaded[n], 16)
            sp.dma_start(table[:, :, :], io["rope"][0:SEQ, 2 * HD:].rearrange("(i p) c -> p i c", p=P))\
                .then_inc(table_loaded, 16)
            sp.dma_start(meta_table[:, :], io["rope"][SEQ:TOK, 2 * HD:]).then_inc(table_loaded, 16)
            load(1, 1)

            def body(j, parity):
                s, g = j + 2, parity
                if valid(s) and not (isinstance(s, int) and s < 2):
                    load(s, g)
                s, g = j, parity
                if valid(s):
                    groups, cols = place(s, g)
                    wait_alone(sp, up_dve, 2 * s + 2, sp_passed)
                    for gg in groups:
                        sp.dma_start(scr["mv"][gg, cols, :, :], vm_st[0:rows_of(s), g, :, :].bitcast(F32))\
                            .then_inc(mv_stored[g], 16)
                s, g = j - 1, 1 - parity
                if valid(s):
                    groups, cols = place(s, g)
                    r = rows_of(s)
                    wait_alone(sp, tp_lo, fill("mkT", s, g)[0] + 1, sp_passed)
                    for gg in groups:
                        for part, tile in enumerate((m_hi, m_lo)):
                            for k, name in enumerate(("mq_t", "mk_t")):
                                sp.dma_start(scr[name][part, gg, :, :, cols].rearrange("h p n -> p h n"),
                                             tile[:, g, k, :, 0:r].bitcast(F32)).then_inc(stored[g], 16)

            steps(sp, body, 1, 1)
            for sem_of, each in ((stored, STORES), (mv_stored, 16)):
                sp.wait_ge(sem_of[0], each * ((N + 1) // 2 + 1))
                sp.wait_ge(sem_of[1], each * (N // 2))

        @block.tensor
        def _(pe):
            pe.wait_ge(ident_ready, 2)

            def turn(kind, s, g, tile):
                n, b = fill(kind, s, g)
                r = rows_of(s)
                at_least(pe, tp_hi, n - 1)
                at_least(pe, tp_lo, n - 1)
                for h in range(HEADS):
                    ins = pe.transpose(tp[0:QK_M, b, h, 0:r], tile[0:r, g, h, :], ident[0:r, 0:r])
                ins.then_inc(tp_filled, 1)

            def body(j, parity):
                s, g = j, parity
                if valid(s):
                    r = rows_of(s)
                    pe.wait_ge(loaded[g], LOADS * (tile_index(s, g) + 1))
                    at_least(pe, up_act, 2 * s)
                    at_least(pe, up_dve, 2 * s)
                    hi, lo = (lambda base: lambda k: lat[:, g, 0, base + k, 0:r]), (lambda base: lambda k: lat[:, g, 1, base + k, 0:r])
                    ready = lambda base: (lambda k: pe.wait_ge(piece_lo, base + k + 1)) if isinstance(s, int) and s == 0 else None
                    split_product(pe, lambda c, w: acc[0:r, c, 0:w], QRK, hi(0), lo(0), uq_hi, uq_lo,
                                  [(0, 384), (384, 768)], ready(0))
                    split_product(pe, lambda c, w: acc[0:r, 2 + c, 0:w], KVRK, hi(QRK), lo(QRK), ukv_hi, ukv_lo,
                                  [(0, 512), (512, 1024)], ready(QRK)).then_inc(up_filled, 1)
                s, g = j - 1, 1 - parity
                if valid(s):
                    pe.wait_ge(rope_done, s + 1)
                    pe.wait_ge(km_done, s + 1)
                    turn("mqT", s, g, qm)
                    turn("mkT", s, g, km)

            steps(pe, body, 1, 1)

        @block.scalar
        def _(act):
            for n, (_, k, raw, hi, _) in enumerate(pieces):
                act.wait_ge(piece_loaded[n], 16)
                act.copy(hi[:, k, :], raw[:, k, :]).then_inc(piece_hi, 1)

            def copy_hi(kind, s, g, out):
                n, b = fill(kind, s, g)
                act.wait_ge(tp_filled, n + 1)
                act.copy(out, tp[0:QK_M, b, :, 0:rows_of(s)]).then_inc(tp_hi, 1)

            def body(j, parity):
                s, g = j, parity
                if valid(s):
                    r = rows_of(s)
                    act.wait_ge(up_filled, s + 1)
                    if not isinstance(s, int) or s >= 2:
                        act.wait_ge(tp_filled, fill("mkT", s - 2, g)[0] + 1)
                        act.wait_ge(mv_stored[g], 16 * tile_index(s, g))
                    act.copy(km[0:r, g, :, 0:NOPE], kv_acc[0:r, :, 0:NOPE]).then_inc(up_act, 1)
                    act.copy(vm_st[0:r, g, :, 0:VD], kv_acc[0:r, :, NOPE:]).then_inc(up_act, 1)
                s, g = j - 1, 1 - parity
                if valid(s):
                    r = rows_of(s)
                    if not isinstance(s, int) or s >= 2:
                        act.wait_ge(stored[g], STORES * tile_index(s, g))
                    copy_hi("mqT", s, g, m_hi[:, g, 0, :, 0:r])
                    copy_hi("mkT", s, g, m_hi[:, g, 1, :, 0:r])

            steps(act, body, 1, 1)

        @block.vector
        def _(dve):
            for n, (_, k, raw, hi, lo) in enumerate(pieces):
                dve.wait_ge(piece_hi, n + 1)
                dve.tensor_tensor(lo[:, k, :], raw[:, k, :], hi[:, k, :].bitcast(F32), ALU.subtract)\
                    .then_inc(piece_lo, 1)
            dve.wait_ge(table_loaded, 32)

            def split_lo(kind, s, g, out, hi):
                n, b = fill(kind, s, g)
                dve.wait_ge(tp_hi, n + 1)
                dve.tensor_tensor(out, tp[0:QK_M, b, :, 0:rows_of(s)], hi.bitcast(F32), ALU.subtract)\
                    .then_inc(tp_lo, 1)

            ROPE_LINKS = 2

            def body(j, parity):
                s, g = j - 1, 1 - parity
                if valid(s):
                    r = rows_of(s)
                    link = Chain(dve, rope_chain, ROPE_LINKS, s)
                    dve.wait_ge(up_dve, 2 * s + 2)
                    if isinstance(s, int) and s == N - 1:
                        cos, sin = meta_table[:, 0:ROT], meta_table[:, ROT:2 * ROT]
                    else:
                        t = table[:, bass.ds(tile_index(s, g), 1), :].rearrange("p o c -> p (o c)")
                        cos, sin = t[:, 0:ROT], t[:, ROT:2 * ROT]
                    rot, a, b = qm[0:r, g, :, NOPE:QK_M], rot_a[0:r, :, :], rot_b[0:r, :, :]
                    (b0, b1), (r0, r1) = rope_halves(b), rope_halves(rot)
                    s0, s1 = rope_halves(spread(sin, 1, HEADS))
                    dve.tensor_tensor(a, rot, spread(cos, 1, HEADS), ALU.mult)
                    link(dve.tensor_tensor(b0, r1, s0, ALU.mult))
                    link(dve.tensor_tensor(b1, r0, s1, ALU.mult))
                    dve.tensor_tensor(rot, a, b, ALU.add).then_inc(rope_done, 1)
                    link.end()
                s, g = j, parity
                if valid(s):
                    r = rows_of(s)
                    dve.wait_ge(up_filled, s + 1)
                    if not isinstance(s, int) or s >= 2:
                        dve.wait_ge(tp_filled, fill("mqT", s - 2, g)[0] + 1)
                    dve.tensor_copy(qm[0:r, g, :, :].rearrange("p (a h) d -> p a (h d)", a=2), acc[0:r, 0:2, 0:384])\
                        .then_inc(up_dve, 1)
                    dve.wait_ge(up_act, 2 * s + 2)
                    dve.tensor_tensor(vm_st[0:r, g, :, VD:], kv_acc[0:r, :, NOPE:], vm_st[0:r, g, :, 0:VD].bitcast(F32),
                                      ALU.subtract).then_inc(up_dve, 1)
                s, g = j - 1, 1 - parity
                if valid(s):
                    r = rows_of(s)
                    split_lo("mqT", s, g, m_lo[:, g, 0, :, 0:r], m_hi[:, g, 0, :, 0:r])
                    split_lo("mkT", s, g, m_lo[:, g, 1, :, 0:r], m_hi[:, g, 1, :, 0:r])

            steps(dve, body, 1, 1)

        @block.gpsimd
        def _(pool):
            identity_matrix(pool, ident, ident_ready)

            def body(j, parity):
                s, g = j - 1, 1 - parity
                if valid(s):
                    r = rows_of(s)
                    wait_alone(pool, k_rot_loaded[g], 16 * (tile_index(s, g) + 1), pool_passed)
                    wait_alone(pool, up_act, 2 * s + 2, pool_passed)
                    pool.tensor_copy(km[0:r, g, :, NOPE:QK_M], spread(k_rot[0:r, g, :], 1, HEADS)).then_inc(km_done, 1)

            steps(pool, body, 1, 1)


def attend(nc, io, scr, mla):
    UNITS = GROUPS * HEADS
    CH = XCH + 1
    BLOCKS = (CH + 1) // 2
    RING = 3
    EARLY = 4 if mla else 0
    scale = (QK_M if mla else HD) ** -0.5
    tag = "m_" if mla else "g_"
    with ExitStack() as ctx:
        def sb(name, shape, dt=F32):
            return ctx.enter_context(nc.sbuf_tensor(tag + name, shape, dt))

        def sem(name):
            return nc.alloc_semaphore(tag + name)

        KD = QK_M if mla else P
        q = sb("q", [KD, 2, 2 if mla else 1, TOK], F32R)
        k = sb("k", [KD, 2, 2, TOK], F32R)
        v = sb("v", [P, 2, CH, 2 * VD], F32R)
        probs, meta_probs = sb("probs", [P, 2, SEQ]), sb("meta_probs", [P, 2, CH, META])
        meta_scores = sb("meta_scores", [P, 2, CH, META])
        meta_max = sb("meta_max", [P, 2, CH])
        peak, bias = sb("peak", [P, 2]), sb("bias", [P, 2])
        sum_x, sum_meta = sb("sum_x", [P, 2, CH]), sb("sum_meta", [P, 2, CH])
        total, inverse = sb("total", [P, 2]), sb("inverse", [P, 2, CH])
        pt_hi, pt_lo = sb("pt_hi", [P, CH, TOK], F32R), sb("pt_lo", [P, CH, TOK], F32R)
        low_half, scales, summed = sb("low_half", [VD, 2, 256]), sb("scales", [VD, 2, 256]), sb("summed", [VD, 2, 256])
        out_hi, out_lo = sb("out_hi", [VD, 2, TOK], F32R), sb("out_lo", [VD, 2, TOK], F32R)
        ident = sb("ident", [P, P])
        s_ps = ctx.enter_context(nc.psum_tensor(tag + "s_ps", [P, 2, SEQ], F32))
        tp = ctx.enter_context(nc.psum_tensor(tag + "tp", [P, RING, 512], F32))
        o_ps = ctx.enter_context(nc.psum_tensor(tag + "o_ps", [P, 512], F32))

        loaded, v_loaded = [sem("loaded0"), sem("loaded1")], [sem("v_loaded0"), sem("v_loaded1")]
        stored = [sem("stored0"), sem("stored1")]
        ident_ready, pool_passed, sp_passed = sem("ident_ready"), sem("pool_passed"), sem("sp_passed")
        pe_passed = sem("pe_passed")
        s_filled, peak_done, bias_done, exp_x_done, exp_done = (sem("s_filled"), sem("peak_done"), sem("bias_done"),
                                                                sem("exp_x_done"), sem("exp_done"))
        total_done, inverse_done = sem("total_done"), sem("inverse_done")
        tp_filled, tp_hi, tp_lo = sem("tp_filled"), sem("tp_hi"), sem("tp_lo")
        o_filled, o_act, o_summed = sem("o_filled"), sem("o_act"), sem("o_summed")
        scaled, out_hi_done, out_done = sem("scaled"), sem("out_hi_done"), sem("out_done")
        block = ctx.enter_context(nc.Block())

        def queries(c):
            return META if c == CH - 1 else P

        def block_of(c):
            return c // 2

        def block_columns(b):
            return slice(256 * b, min(256 * (b + 1), TOK))

        def block_width(b):
            return META if b == BLOCKS - 1 else 256

        kinds = []
        for c in range(CH):
            kinds += [("x", c, 0), ("x", c, 1)]
            if c % 2 == 1 or c == CH - 1:
                kinds.append(("meta", block_of(c)))
            if c == CH - 3:
                kinds.append(("scores", 0))
        FILLS = len(kinds)
        assert FILLS % RING == 0

        def fill(u, *kind):
            idx = kinds.index(kind)
            if is_last(u) and idx > kinds.index(("scores", 0)):
                idx -= 1
            return FILLS * u + 1 + idx, (1 + idx) % RING

        def score_fill(u):
            if isinstance(u, int) and u == 0:
                return 0, 0
            n, b = fill(u - 1, "scores", 0)
            return n, b

        def chunk_number(u, c, parity):
            return CH * u + c, (CH * parity + c) % 2

        def block_number(u, b, parity):
            return BLOCKS * u + b, (BLOCKS * parity + b) % 2

        def units(eng, body):
            for u in range(2):
                body(u, u)
            with eng.Fori(1, (UNITS - 2) // 2) as i:
                for p in range(2):
                    body(2 * i + p, p)
            for u in range(UNITS - 2, UNITS):
                body(u, u % 2)

        def is_last(u):
            return isinstance(u, int) and u == UNITS - 1

        def head_and_group(u, parity):
            return (u // 2 if isinstance(u, int) else (u - parity) // 2), parity

        LOADS = 16 * (4 if mla else 3)

        @block.sync
        def _(sp):
            def load(u, p):
                h, g = head_and_group(u, p)
                wait_alone(sp, o_filled, BLOCKS * (u - 1), sp_passed)
                one = bass.ds(h, 1)
                if mla:
                    for part in range(2):
                        sp.dma_start(q[:, p, part, :].bitcast(F32), scr["mq_t"][part, g, one, :, :].rearrange("o p n -> (o p) n"))\
                            .then_inc(loaded[p], 16)
                        sp.dma_start(k[:, p, part, :].bitcast(F32), scr["mk_t"][part, g, one, :, :].rearrange("o p n -> (o p) n"))\
                            .then_inc(loaded[p], 16)
                    values, hh = scr["mv"], one
                else:
                    kv = bass.ds(h // (HEADS // KV), 1)
                    sp.dma_start(q[:, p, 0, :].bitcast(F32), scr["gq_t"][g, one, :, :].rearrange("o p n -> (o p) n"))\
                        .then_inc(loaded[p], 16)
                    for part in range(2):
                        sp.dma_start(k[:, p, part, :].bitcast(F32), scr["gk_t"][part, g, kv, :, :].rearrange("o p n -> (o p) n"))\
                            .then_inc(loaded[p], 16)
                    values, hh = scr["gv"], kv
                sp.dma_start(v[:, p, 0:XCH, :].bitcast(F32),
                             values[g, 0:SEQ, hh, :].rearrange("(i p) o n -> p i (o n)", p=P)).then_inc(v_loaded[p], 16)
                sp.dma_start(v[0:META, p, XCH, :].bitcast(F32),
                             values[g, SEQ:TOK, hh, :].rearrange("p o n -> p (o n)")).then_inc(v_loaded[p], 16)

            def store(u, p):
                h, g = head_and_group(u, p)
                wait_alone(sp, out_done, BLOCKS * (u + 1), sp_passed)
                for part, tile in enumerate((out_hi, out_lo)):
                    sp.dma_start(scr["o_t"][1 if mla else 0, part, g, bass.ds(h * VD, VD), :],
                                 tile[:, p, :].bitcast(F32)).then_inc(stored[p], 16)

            load(0, 0)

            def body(u, p):
                if not is_last(u):
                    load(u + 1, 1 - p)
                if not (isinstance(u, int) and u == 0):
                    store(u - 1, 1 - p)

            units(sp, body)
            store(UNITS - 1, (UNITS - 1) % 2)
            for p in range(2):
                sp.wait_ge(stored[p], 32 * (UNITS // 2))

        @block.tensor
        def _(pe):
            pe.wait_ge(ident_ready, 2)
            passes = [(0, 0), (0, 1), (1, 0)] if mla else [(0, 0), (0, 1)]

            def bank_free(n, alone=False):
                at_least(pe, tp_hi, n - RING + 1)
                if alone:
                    wait_alone(pe, tp_lo, n - RING + 1, pe_passed)
                else:
                    at_least(pe, tp_lo, n - RING + 1)

            def loads_of(u, p):
                return (u if isinstance(u, int) else u - p) // 2 + 1

            def wait_loaded(u, p):
                pe.wait_ge(loaded[p], LOADS * loads_of(u, p))

            def meta_keys(u, p, chunks):
                n, bank = score_fill(u)
                wait_loaded(u, p)
                bank_free(n)
                for c in chunks:
                    r = queries(c)
                    for at, (a, b) in enumerate(passes):
                        ins = pe.matmul(tp[0:r, bank, c * META:(c + 1) * META], q[:, p, a, c * P:c * P + r],
                                        k[:, p, b, SEQ:TOK], start=(at == 0), stop=(at == len(passes) - 1))
                if c == CH - 1:
                    ins.then_inc(tp_filled, 1)

            def scores(u, p, c):
                n, buf = chunk_number(u, c, p)
                r = queries(c)
                if c == 0:
                    wait_loaded(u, p)
                at_least(pe, exp_x_done, n - 1)
                for at, (a, b) in enumerate(passes):
                    for half in range(2):
                        ins = pe.matmul(s_ps[0:r, buf, half * 512:(half + 1) * 512], q[:, p, a, c * P:c * P + r],
                                        k[:, p, b, half * 512:(half + 1) * 512],
                                        start=(at == 0), stop=(at == len(passes) - 1))
                ins.then_inc(s_filled, 1)

            def transposes(u, p, c):
                n, buf = chunk_number(u, c, p)
                r = queries(c)
                pe.wait_ge(exp_done, n + 1)
                for half in range(2):
                    f, bank = fill(u, "x", c, half)
                    bank_free(f, r < P)
                    for t in range(4):
                        at = (half * 4 + t) * P
                        ins = pe.transpose(tp[:, bank, t * P:t * P + r], probs[0:r, buf, at:at + P], ident[0:r, 0:r])
                    ins.then_inc(tp_filled, 1)
                if c % 2 == 1 or c == CH - 1:
                    f, bank = fill(u, "meta", block_of(c))
                    bank_free(f, True)
                    for cc in range(block_of(c) * 2, c + 1):
                        r = queries(cc)
                        ins = pe.transpose(tp[0:META, bank, (cc % 2) * P:(cc % 2) * P + r],
                                           meta_probs[0:r, p, cc, :], ident[0:r, 0:r])
                    ins.then_inc(tp_filled, 1)

            def values(u, p, b, part):
                n, buf = block_number(u, b, p)
                w = block_width(b)
                pe.wait_ge(tp_lo, fill(u, "meta", b)[0] + 1)
                if part == 0:
                    if b == 0:
                        pe.wait_ge(v_loaded[p], 32 * loads_of(u, p))
                    at_least(pe, o_summed, n)
                for kk in (range(0, 4) if part == 0 else range(4, CH)):
                    kr = META if kk == CH - 1 else P
                    for tile in (pt_hi, pt_lo):
                        ins = pe.matmul(o_ps[:, 0:w], v[0:kr, p, kk, :], tile[0:kr, kk, block_columns(b)],
                                        start=(kk == 0 and tile is pt_hi), stop=(kk == CH - 1 and tile is pt_lo))
                if part == 1:
                    last = min(2 * b + 1, CH - 1)
                    wait_alone(pe, inverse_done, chunk_number(u, last, p)[0] + 1, pe_passed)
                    for c in range(2 * b, last + 1):
                        r = queries(c)
                        ins = pe.transpose(o_ps[0:VD, 256 + (c % 2) * P:256 + (c % 2) * P + r],
                                           inverse[0:r, p, c:c + 1].broadcast_to((r, VD)), ident[0:r, 0:r])
                    ins.then_inc(o_filled, 1)

            scores(0, 0, 0)
            meta_keys(0, 0, range(CH))
            scores(0, 0, 1)

            def body(u, p):
                first = isinstance(u, int) and u == 0
                for c in range(CH):
                    if c < CH - 2:
                        scores(u, p, c + 2)
                    elif not is_last(u):
                        scores(u + 1, 1 - p, c + 2 - CH)
                    if EARLY and c == CH - 3 and not is_last(u):
                        meta_keys(u + 1, 1 - p, range(EARLY))
                    transposes(u, p, c)
                    if c == CH - 3 and not is_last(u):
                        meta_keys(u + 1, 1 - p, range(EARLY, CH))
                    if c == 0 and not first:
                        values(u - 1, 1 - p, BLOCKS - 2, 1)
                    elif c == 1 and not first:
                        values(u - 1, 1 - p, BLOCKS - 1, 0)
                        values(u - 1, 1 - p, BLOCKS - 1, 1)
                    elif c >= 2:
                        values(u, p, block_of(c) - 1, c % 2)

            units(pe, body)
            values(UNITS - 1, (UNITS - 1) % 2, BLOCKS - 2, 1)
            values(UNITS - 1, (UNITS - 1) % 2, BLOCKS - 1, 0)
            values(UNITS - 1, (UNITS - 1) % 2, BLOCKS - 1, 1)

        def meta_copy(act, u, p):
            n, bank = score_fill(u)
            act.wait_ge(tp_filled, n + 1)
            act.copy(meta_scores[:, p, 0:XCH, :].rearrange("p c m -> p (c m)"), tp[:, bank, 0:XCH * META])
            act.copy(meta_scores[0:META, p, XCH, :], tp[0:META, bank, XCH * META:CH * META]).then_inc(tp_hi, 1)

        def blocks_done(u, p, c):
            if c < 2:
                return [] if isinstance(u, int) and u == 0 else [(u - 1, 1 - p, BLOCKS - 2 + c)]
            return [(u, p, block_of(c) - 1)] if c % 2 == 1 else []

        @block.scalar
        def _(act):
            def softmax(u, p, c):
                n, buf = chunk_number(u, c, p)
                r = queries(c)
                act.wait_ge(bias_done, n + 1)
                if not (isinstance(u, int) and u == 0 and c < 2):
                    uu, cc = (u, c - 2) if c >= 2 else (u - 1, c - 2 + CH)
                    act.wait_ge(tp_filled, fill(uu, "x", cc, 1)[0] + 1)
                act.activation(probs[0:r, buf, :], s_ps[0:r, buf, :], ACT.Exp, bias=bias[0:r, buf:buf + 1],
                               scale=scale, accum_out=sum_x[0:r, p, c:c + 1]).then_inc(exp_x_done, 1)
                act.activation(meta_probs[0:r, p, c, :], meta_scores[0:r, p, c, :], ACT.Exp,
                               bias=bias[0:r, buf:buf + 1], scale=scale,
                               accum_out=sum_meta[0:r, p, c:c + 1]).then_inc(exp_done, 1)

            def hi(u, p, c):
                r = queries(c)
                bn, bb = block_number(u, block_of(c), p)
                if c % 2 == 0:
                    at_least(act, o_filled, bn - BLOCKS + 1)
                for half in range(2):
                    f, bank = fill(u, "x", c, half)
                    act.wait_ge(tp_filled, f + 1)
                    act.copy(pt_hi[:, half * 4:half * 4 + 4, c * P:c * P + r],
                             tp[:, bank, :].rearrange("p (t n) -> p t n", t=4)[:, :, 0:r]).then_inc(tp_hi, 1)
                if c % 2 == 1 or c == CH - 1:
                    w = block_width(block_of(c))
                    f, bank = fill(u, "meta", block_of(c))
                    act.wait_ge(tp_filled, f + 1)
                    act.copy(pt_hi[0:META, CH - 1, block_columns(block_of(c))], tp[0:META, bank, 0:w]).then_inc(tp_hi, 1)

            def evacuate(u, p, b):
                bn, bb = block_number(u, b, p)
                w = block_width(b)
                act.wait_ge(o_filled, bn + 1)
                at_least(act, scaled, bn - 1)
                act.copy(low_half[:, bb, 0:w], o_ps[VD:P, 0:w])
                act.copy(scales[:, bb, 0:w], o_ps[0:VD, 256:256 + w]).then_inc(o_act, 1)

            meta_copy(act, 0, 0)
            softmax(0, 0, 0)

            def body(u, p):
                for c in range(CH):
                    if c < CH - 1:
                        softmax(u, p, c + 1)
                    elif not is_last(u):
                        softmax(u + 1, 1 - p, 0)
                    if c == CH - 2 and not is_last(u):
                        meta_copy(act, u + 1, 1 - p)
                    hi(u, p, c)
                    for done in blocks_done(u, p, c):
                        evacuate(*done)

            units(act, body)
            evacuate(UNITS - 1, (UNITS - 1) % 2, BLOCKS - 2)
            evacuate(UNITS - 1, (UNITS - 1) % 2, BLOCKS - 1)

        @block.vector
        def _(dve):
            def meta_peak(u, p):
                n, bank = score_fill(u)
                dve.wait_ge(tp_hi, n + 1)
                dve.tensor_reduce(meta_max[:, p, 0:XCH], tp[:, bank, 0:XCH * META].rearrange("p (c m) -> p c m", m=META),
                                  AX_X, ALU.max)
                dve.tensor_reduce(meta_max[0:META, p, XCH:CH], tp[0:META, bank, XCH * META:CH * META], AX_X, ALU.max)\
                    .then_inc(tp_lo, 1)

            def peaks(u, p, c):
                n, buf = chunk_number(u, c, p)
                r = queries(c)
                dve.wait_ge(s_filled, n + 1)
                at_least(dve, exp_done, n - 1)
                dve.tensor_reduce(peak[0:r, buf:buf + 1], s_ps[0:r, buf, :], AX_X, ALU.max).then_inc(peak_done, 1)

            def biases(u, p, c):
                n, buf = chunk_number(u, c, p)
                r = queries(c)
                dve.wait_ge(peak_done, n + 1)
                if c == 0:
                    dve.wait_ge(tp_lo, score_fill(u)[0] + 1)
                dve.tensor_scalar(bias[0:r, buf:buf + 1], peak[0:r, buf:buf + 1], meta_max[0:r, p, c:c + 1], -scale,
                                  ALU.max, ALU.mult).then_inc(bias_done, 1)

            def totals(u, p, c):
                n, buf = chunk_number(u, c, p)
                r = queries(c)
                dve.wait_ge(exp_done, n + 1)
                dve.tensor_tensor(total[0:r, buf:buf + 1], sum_x[0:r, p, c:c + 1], sum_meta[0:r, p, c:c + 1], ALU.add)\
                    .then_inc(total_done, 1)

            def inverses(u, p, c):
                n, buf = chunk_number(u, c, p)
                r = queries(c)
                dve.wait_ge(total_done, n + 1)
                dve.reciprocal(inverse[0:r, p, c:c + 1], total[0:r, buf:buf + 1]).then_inc(inverse_done, 1)

            def lo(u, p, c):
                r = queries(c)
                bn, bb = block_number(u, block_of(c), p)
                for half in range(2):
                    f, bank = fill(u, "x", c, half)
                    dve.wait_ge(tp_hi, f + 1)
                    span = (slice(None), slice(half * 4, half * 4 + 4), slice(c * P, c * P + r))
                    dve.tensor_tensor(pt_lo[span], tp[:, bank, :].rearrange("p (t n) -> p t n", t=4)[:, :, 0:r],
                                      pt_hi[span].bitcast(F32), ALU.subtract).then_inc(tp_lo, 1)
                if c % 2 == 1 or c == CH - 1:
                    w = block_width(block_of(c))
                    span = (slice(0, META), CH - 1, block_columns(block_of(c)))
                    f, bank = fill(u, "meta", block_of(c))
                    dve.wait_ge(tp_hi, f + 1)
                    dve.tensor_tensor(pt_lo[span], tp[0:META, bank, 0:w], pt_hi[span].bitcast(F32),
                                      ALU.subtract).then_inc(tp_lo, 1)

            def sum_halves(u, p, b):
                bn, bb = block_number(u, b, p)
                w = block_width(b)
                at_least(dve, out_done, bn - 1)
                dve.wait_ge(o_act, bn + 1)
                dve.tensor_tensor(summed[:, bb, 0:w], o_ps[0:VD, 0:w], low_half[:, bb, 0:w], ALU.add)\
                    .then_inc(o_summed, 1)

            peaks(0, 0, 0)
            meta_peak(0, 0)
            biases(0, 0, 0)
            peaks(0, 0, 1)
            biases(0, 0, 1)

            def body(u, p):
                for c in range(CH):
                    if c < CH - 2:
                        peaks(u, p, c + 2)
                    elif not is_last(u):
                        if c == CH - 2:
                            meta_peak(u + 1, 1 - p)
                        peaks(u + 1, 1 - p, c + 2 - CH)
                    totals(u, p, c)
                    if c < CH - 2:
                        biases(u, p, c + 2)
                    elif not is_last(u):
                        biases(u + 1, 1 - p, c + 2 - CH)
                    inverses(u, p, c)
                    lo(u, p, c)
                    for done in blocks_done(u, p, c):
                        sum_halves(*done)
            units(dve, body)
            sum_halves(UNITS - 1, (UNITS - 1) % 2, BLOCKS - 2)
            sum_halves(UNITS - 1, (UNITS - 1) % 2, BLOCKS - 1)

        @block.gpsimd
        def _(pool):
            identity_matrix(pool, ident, ident_ready)

            def finish_block(u, p, b):
                bn, bb = block_number(u, b, p)
                w = block_width(b)
                cols = slice(b * 256, b * 256 + w)
                if b == 0:
                    if not isinstance(u, int) or u >= 2:
                        wait_alone(pool, stored[p], 32 * ((u if isinstance(u, int) else u - p) // 2), pool_passed)
                wait_alone(pool, o_summed, bn + 1, pool_passed)
                pool.tensor_tensor(summed[:, bb, 0:w], summed[:, bb, 0:w], scales[:, bb, 0:w], ALU.mult)\
                    .then_inc(scaled, 1)
                wait_alone(pool, scaled, bn + 1, pool_passed)
                pool.tensor_copy(out_hi[:, p, cols], summed[:, bb, 0:w]).then_inc(out_hi_done, 1)
                pool.wait_ge(out_hi_done, bn + 1)
                pool.tensor_tensor(out_lo[:, p, cols], summed[:, bb, 0:w], out_hi[:, p, cols].bitcast(F32), ALU.subtract)\
                    .then_inc(out_done, 1)

            def body(u, p):
                for b in range(BLOCKS):
                    finish_block(u, p, b)

            units(pool, body)


def mix(nc, io, scr):
    WIDE = TOK // 2
    NB = 2
    W = WIDE // NB
    OK = HEADS * HD // P
    HALF_K = DK + OK
    GATES = TOKEN_COLS
    with ExitStack() as ctx:
        def sb(name, shape, dt=F32):
            return ctx.enter_context(nc.sbuf_tensor("c_" + name, shape, dt))

        def sem(name):
            return nc.alloc_semaphore("c_" + name)

        tokens = sb("tokens", [P, 2, 2, DK + 2 * OK, WIDE], F32R)
        raw = sb("raw", [P, 2, HALF_K, P])
        w_hi, w_lo = sb("w_hi", [P, 2, 2, HALF_K, P], F32R), sb("w_lo", [P, 2, 2, HALF_K, P], F32R)
        gate = sb("gate", [P, 2, W])
        prod = sb("prod", [P, 2, W])
        mixed = sb("mixed", [P, W])
        out_hi, out_lo = sb("out_hi", [P, WIDE], F32R), sb("out_lo", [P, WIDE], F32R)
        acc = ctx.enter_context(nc.psum_tensor("c_acc", [P, 2, 4, 512], F32))

        tokens_loaded = [[[sem(f"tokens_loaded{p}{b}{k}") for k in range(3)] for b in range(NB)] for p in range(2)]
        piece_loaded = [sem("piece_loaded0"), sem("piece_loaded1")]
        piece_hi, piece_lo = sem("piece_hi"), sem("piece_lo")
        acc_filled, gates_done, prod_done, sum_done, hi_done, lo_done = (
            sem("acc_filled"), sem("gates_done"), sem("prod_done"), sem("sum_done"), sem("hi_done"), sem("lo_done"))
        stored, sp_passed = sem("stored"), sem("sp_passed")
        block = ctx.enter_context(nc.Block())
        PASSES = GROUPS * 2

        def units(eng, body):
            body(0, 0, 0)
            body(0, 1, 1)
            for t in range(PASSES):
                with eng.Fori(1 if t == 0 else 0, DK // 2) as i:
                    for parity in range(2):
                        body(t, 2 * i + parity, parity)

        @block.sync
        def _(sp):
            def load_tokens(t, part_of):
                g, h = t // 2, t % 2
                b, k = part_of // 3, part_of % 3
                cols = slice(h * WIDE + b * W, h * WIDE + (b + 1) * W)
                for part in range(2):
                    if k == 0:
                        tiles, src = slice(0, DK), scr["hn_t"][part, g, :, :, cols]
                    else:
                        tiles = slice(DK + (k - 1) * OK, DK + k * OK)
                        src = scr["o_t"][k - 1, part, g, :, cols].rearrange("(k p) n -> p k n", p=P)
                    sp.dma_start(tokens[:, t % 2, part, tiles, b * W:(b + 1) * W].bitcast(F32), src)\
                        .then_inc(tokens_loaded[t % 2][b][k], 16)

            def load_pieces(t, m):
                for mixer in range(2):
                    n = 2 * (DK * t + m) + mixer
                    wait_alone(sp, piece_lo, n - 1, sp_passed)
                    sp.dma_start(raw[:, mixer, 0:DK, :],
                                 io["w_in"][0, :, bass.ds(GATES + mixer * D + m * P, P)].rearrange("(k p) n -> p k n", p=P))\
                        .then_inc(piece_loaded[mixer], 16)
                    sp.dma_start(raw[:, mixer, DK:, :],
                                 io["w_o_mla" if mixer else "w_o_gqa"][0, :, bass.ds(m * P, P)].rearrange("(k p) n -> p k n", p=P))\
                        .then_inc(piece_loaded[mixer], 16)

            load_pieces(0, 0)
            for part_of in range(3 * NB):
                load_tokens(0, part_of)
                if part_of == 2:
                    load_pieces(0, 1)
            for t in range(PASSES):
                def store(m):
                    n = DK * t + m
                    wait_alone(sp, lo_done, NB * (n + 1), sp_passed)
                    for part, tile in enumerate((out_hi, out_lo)):
                        sp.dma_start(scr["mix_t"][part, t // 2, :, bass.ds(m, 1), (t % 2) * WIDE:(t % 2 + 1) * WIDE]
                                     .rearrange("p o n -> p (o n)"), tile[:, :].bitcast(F32)).then_inc(stored, 16)

                for m in range(3):
                    if t > 0 or m > 0:
                        load_pieces(t, m + 1)
                    if t + 1 < PASSES:
                        if t > 0 and m == 0:
                            sp.wait_ge(acc_filled, NB * DK * t)
                        for part_of in range(m * NB, (m + 1) * NB):
                            load_tokens(t + 1, part_of)
                    store(m)
                with sp.Fori(3, DK - 1) as m:
                    load_pieces(t, m + 1)
                    store(m)
                if t + 1 < PASSES:
                    load_pieces(t + 1, 0)
                store(DK - 1)
            sp.wait_ge(stored, 32 * DK * PASSES)

        @block.tensor
        def _(pe):
            def body(t, m, parity):
                n = DK * t + m
                pe.wait_ge(piece_lo, 2 * n + 2)
                for b in range(NB):
                    pe.wait_ge(tokens_loaded[t % 2][b][0], 32 * (t // 2 + 1))
                    cols = slice(b * W, (b + 1) * W)
                    at_least(pe, prod_done, NB * n + b - 1)
                    for mixer in range(2):
                        for k in range(DK):
                            for at, (w, part) in enumerate(((w_hi, 0), (w_hi, 1), (w_lo, 0))):
                                pe.matmul(acc[:, b, mixer, 0:W], w[:, parity, mixer, k, :],
                                          tokens[:, t % 2, part, k, cols],
                                          start=(k == 0 and at == 0), stop=(k == DK - 1 and at == 2))
                    for mixer in range(2):
                        pe.wait_ge(tokens_loaded[t % 2][b][1 + mixer], 32 * (t // 2 + 1))
                        for k in range(OK):
                            for at, (w, part) in enumerate(((w_hi, 0), (w_hi, 1), (w_lo, 0))):
                                ins = pe.matmul(acc[:, b, 2 + mixer, 0:W], w[:, parity, mixer, DK + k, :],
                                                tokens[:, t % 2, part, DK + mixer * OK + k, cols],
                                                start=(k == 0 and at == 0), stop=(k == OK - 1 and at == 2))
                    ins.then_inc(acc_filled, 1)

            units(pe, body)

        @block.scalar
        def _(act):
            def split_pieces(t, m, parity):
                for mixer in range(2):
                    n = 2 * (DK * t + m) + mixer
                    act.wait_ge(piece_loaded[mixer], 32 * (DK * t + m + 1))
                    act.copy(w_hi[:, parity, mixer, :, :], raw[:, mixer, :, :]).then_inc(piece_hi, 1)

            def gates(t, m, b):
                n = NB * (DK * t + m) + b
                act.wait_ge(acc_filled, n + 1)
                at_least(act, prod_done, n)
                act.activation(gate[:, :, :], acc[:, b, 0:2, 0:W], ACT.Sigmoid).then_inc(gates_done, 1)

            def hi(t, m, b):
                n = NB * (DK * t + m) + b
                act.wait_ge(sum_done, n + 1)
                at_least(act, stored, 32 * (DK * t + m))
                act.copy(out_hi[:, b * W:(b + 1) * W], mixed[:, :]).then_inc(hi_done, 1)

            split_pieces(0, 0, 0)

            for t in range(PASSES):
                def body(m, parity, last):
                    if not last:
                        at_least(act, acc_filled, NB * (DK * t + m))
                        split_pieces(t, m + 1, 1 - parity)
                    elif t + 1 < PASSES:
                        act.wait_ge(acc_filled, NB * (DK * t + m))
                        split_pieces(t + 1, 0, 0)
                    for b in range(NB):
                        gates(t, m, b)
                        hi(t, m, b)
                if t == 0:
                    body(0, 0, False)
                    body(1, 1, False)
                with act.Fori(1 if t == 0 else 0, DK // 2 - 1) as i:
                    for parity in range(2):
                        body(2 * i + parity, parity, False)
                body(DK - 2, 0, False)
                body(DK - 1, 1, True)

        @block.vector
        def _(dve):
            def split_pieces(t, m, parity):
                for mixer in range(2):
                    n = 2 * (DK * t + m) + mixer
                    dve.wait_ge(piece_hi, n + 1)
                    dve.tensor_tensor(w_lo[:, parity, mixer, :, :], raw[:, mixer, :, :],
                                      w_hi[:, parity, mixer, :, :].bitcast(F32), ALU.subtract).then_inc(piece_lo, 1)

            def combine(t, m, b):
                n = NB * (DK * t + m) + b
                dve.wait_ge(gates_done, n + 1)
                dve.tensor_tensor(prod[:, :, :], gate[:, :, :], acc[:, b, 2:4, 0:W], ALU.mult).then_inc(prod_done, 1)
                dve.wait_ge(prod_done, n + 1)
                at_least(dve, hi_done, n)
                dve.tensor_tensor(mixed[:, :], prod[:, 0, :], prod[:, 1, :], ALU.add).then_inc(sum_done, 1)
                dve.wait_ge(hi_done, n + 1)
                dve.tensor_tensor(out_lo[:, b * W:(b + 1) * W], mixed[:, :], out_hi[:, b * W:(b + 1) * W].bitcast(F32),
                                  ALU.subtract).then_inc(lo_done, 1)

            split_pieces(0, 0, 0)
            for t in range(PASSES):
                def body(m, parity, last):
                    if not last:
                        split_pieces(t, m + 1, 1 - parity)
                    elif t + 1 < PASSES:
                        split_pieces(t + 1, 0, 0)
                    for b in range(NB):
                        combine(t, m, b)
                if t == 0:
                    body(0, 0, False)
                    body(1, 1, False)
                with dve.Fori(1 if t == 0 else 0, DK // 2 - 1) as i:
                    for parity in range(2):
                        body(2 * i + parity, parity, False)
                body(DK - 2, 0, False)
                body(DK - 1, 1, True)


def residual(nc, io, scr):
    N = STEPS
    BOTH = GROUPS * META
    with ExitStack() as ctx:
        def sb(name, shape, dt=F32):
            return ctx.enter_context(nc.sbuf_tensor("r_" + name, shape, dt))

        def sem(name):
            return nc.alloc_semaphore("r_" + name)

        raw = sb("raw", [P, DK, D])
        w_hi, w_lo = sb("w_hi", [P, DK, D], F32R), sb("w_lo", [P, DK, D], F32R)
        router = sb("router", [P, DK, E])
        gain = sb("gain", [P, D])
        ident = sb("ident", [P, P])
        mt = sb("mt", [P, 2, 2, DK, P], F32R)
        x = sb("x", [P, 2, D])
        h = sb("h", [P, 2, D])
        unused = sb("unused", [P, D])
        t_tile = sb("t_tile", [P, 2, D])
        t_t = sb("t_t", [P, DK, P])
        mean, rs = sb("mean", [P, 1]), sb("rs", [P, 3, 1])
        peak, total = sb("peak", [P, 1]), sb("total", [P, 2])
        aff = sb("aff", [P, E])
        aff_rows = sb("aff_rows", [E, 2, P])
        acc = ctx.enter_context(nc.psum_tensor("r_acc", [P, 2, D], F32))
        tp = ctx.enter_context(nc.psum_tensor("r_tp", [P, DK, P], F32))
        lg = ctx.enter_context(nc.psum_tensor("r_lg", [P, 512], F32))
        at = ctx.enter_context(nc.psum_tensor("r_at", [E, 512], F32))

        piece_loaded = [sem(f"piece_loaded{k}") for k in range(DK)]
        piece_hi, piece_lo, gain_loaded, router_loaded = sem("piece_hi"), sem("piece_lo"), sem("gain_loaded"), sem("router_loaded")
        ident_ready, sp_passed, pe_passed = sem("ident_ready"), sem("sp_passed"), sem("pe_passed")
        loaded = [sem("loaded0"), sem("loaded1")]
        acc_filled, h_done, squared, chain, t_done = sem("acc_filled"), sem("h_done"), sem("squared"), sem("chain"), sem("t_done")
        tp_filled, t_copied, lg_filled = sem("tp_filled"), sem("t_copied"), sem("lg_filled")
        peak_done, exp_done, total_done, aff_done = sem("peak_done"), sem("exp_done"), sem("total_done"), sem("aff_done")
        at_filled, at_copied = sem("at_filled"), sem("at_copied")
        stored, aff_stored = [sem("stored0"), sem("stored1")], [sem("aff_stored0"), sem("aff_stored1")]
        block = ctx.enter_context(nc.Block())

        def rows(s):
            return BOTH if isinstance(s, int) and s == N - 1 else P

        def row_range(s, g):
            if isinstance(s, int) and s == N - 1:
                return slice(GROUPS * SEQ, GROUPS * TOK)
            return bass.ds(g * SEQ + tile_index(s, g) * P, P)

        LOADS = 16 * 3

        @block.sync
        def _(sp):
            def load(s, g):
                wait_alone(sp, h_done, s - 1, sp_passed)
                if isinstance(s, int) and s == N - 1:
                    for gg in range(GROUPS):
                        for part in range(2):
                            sp.dma_start(mt[:, g, part, :, gg * META:(gg + 1) * META].bitcast(F32),
                                         scr["mix_t"][part, gg, :, :, SEQ:TOK]).then_inc(loaded[g], 16)
                        sp.dma_start(x[gg * META:(gg + 1) * META, g, :], io["meta_tokens"]).then_inc(loaded[g], 16)
                else:
                    cols = bass.ds(tile_index(s, g) * P, P)
                    for part in range(2):
                        sp.dma_start(mt[:, g, part, :, :].bitcast(F32), scr["mix_t"][part, g, :, :, cols])\
                            .then_inc(loaded[g], 16)
                    sp.dma_start(x[:, g, :], io["x_prompt" if g == 0 else "x_sample"][0, cols, :])\
                        .then_inc(loaded[g], 16)

            load(0, 0)
            for k in range(DK):
                sp.dma_start(raw[:, k, :], io["w_out"][0, k * P:(k + 1) * P, :]).then_inc(piece_loaded[k], 16)
            load(1, 1)
            sp.dma_start(gain[:, :], spread(io["ffn_norm"][0, :], 0, P)).then_inc(gain_loaded, 16)
            sp.dma_start(router[:, :, :], io["w_router"][0].rearrange("(k p) e -> p k e", p=P)).then_inc(router_loaded, 16)

            def body(j, parity):
                s, g = j + 1, 1 - parity
                if valid(s) and not (isinstance(s, int) and s < 2):
                    load(s, g)
                s, g = j - 1, 1 - parity
                if valid(s):
                    r = rows(s)
                    wait_alone(sp, h_done, s + 1, sp_passed)
                    sp.dma_start(scr["h_rows"][row_range(s, g), :], h[0:r, g, :]).then_inc(stored[g], 16)
                    wait_alone(sp, t_done, s + 1, sp_passed)
                    sp.dma_start(scr["t_rows"][row_range(s, g), :], t_tile[0:r, g, :]).then_inc(stored[g], 16)
                s, g = j - 3, 1 - parity
                if valid(s):
                    wait_alone(sp, at_copied, s + 1, sp_passed)
                    if isinstance(s, int) and s == N - 1:
                        for gg in range(GROUPS):
                            sp.dma_start(scr["aff_t"][gg * E:(gg + 1) * E, 0:META],
                                         aff_rows[:, g, gg * META:(gg + 1) * META]).then_inc(aff_stored[g], 16)
                    else:
                        sp.dma_start(scr["aff_t"][g * E:(g + 1) * E, bass.ds(META + tile_index(s, g) * P, P)],
                                     aff_rows[:, g, :]).then_inc(aff_stored[g], 16)

            steps(sp, body, 1, 3)
            sp.wait_ge(stored[0], 32 * ((N + 1) // 2))
            sp.wait_ge(stored[1], 32 * (N // 2))
            sp.wait_ge(aff_stored[0], 16 * ((N + 1) // 2 + 1))
            sp.wait_ge(aff_stored[1], 16 * (N // 2))

        @block.tensor
        def _(pe):
            pe.wait_ge(ident_ready, 2)

            def body(j, parity):
                s, g = j, parity
                if valid(s):
                    r = rows(s)
                    total_loads = LOADS * (tile_index(s, g) + 1) + (LOADS if isinstance(s, int) and s == N - 1 else 0)
                    pe.wait_ge(loaded[g], total_loads)
                    at_least(pe, h_done, s - 1)

                    def piece_ready(k):
                        pe.wait_ge(piece_lo, k + 1)
                    split_product(pe, lambda c, w: acc[0:r, g, c * 512:(c + 1) * 512], DK,
                                  lambda k: mt[:, g, 0, k, 0:r], lambda k: mt[:, g, 1, k, 0:r], w_hi, w_lo,
                                  [(0, 512), (512, 1024)],
                                  piece_ready if isinstance(s, int) and s == 0 else None).then_inc(acc_filled, 1)
                s, g = j - 2, parity
                if valid(s):
                    r = rows(s)
                    if isinstance(s, int) and s == 0:
                        pe.wait_ge(router_loaded, 16)
                    pe.wait_ge(t_copied, s + 1)
                    at_least(pe, aff_done, s)
                    for k in range(DK):
                        ins = pe.matmul(lg[0:r, 0:E], t_t[:, k, 0:r], router[:, k, :], start=(k == 0), stop=(k == DK - 1))
                    ins.then_inc(lg_filled, 1)
                s, g = j - 3, 1 - parity
                if valid(s):
                    r = rows(s)
                    pe.wait_ge(aff_done, s + 1)
                    wait_alone(pe, at_copied, s, pe_passed)
                    pe.transpose(at[:, 0:r], aff[0:r, :], ident[0:r, 0:r]).then_inc(at_filled, 1)
                s, g = j - 1, 1 - parity
                if valid(s):
                    r = rows(s)
                    pe.wait_ge(t_done, s + 1)
                    at_least(pe, t_copied, s)
                    for k in range(DK):
                        ins = pe.transpose(tp[:, k, 0:r], t_tile[0:r, g, k * P:(k + 1) * P], ident[0:r, 0:r])
                    ins.then_inc(tp_filled, 1)

            steps(pe, body, 1, 3)

        @block.scalar
        def _(act):
            for k in range(DK):
                act.wait_ge(piece_loaded[k], 16)
                act.copy(w_hi[:, k, :], raw[:, k, :]).then_inc(piece_hi, 1)

            def body(j, parity):
                s, g = j - 2, parity
                if valid(s):
                    r = rows(s)
                    at_least(act, at_filled, s)
                    act.wait_ge(peak_done, s + 1)
                    act.activation(aff[0:r, :], lg[0:r, 0:E], ACT.Exp, bias=peak[0:r, :],
                                   accum_out=total[0:r, 0:1]).then_inc(exp_done, 1)
                s, g = j - 3, 1 - parity
                if valid(s):
                    r = rows(s)
                    act.wait_ge(at_filled, s + 1)
                    if not isinstance(s, int) or s >= 2:
                        act.wait_ge(aff_stored[g], 16 * tile_index(s, g))
                    act.copy(aff_rows[:, g, 0:r], at[:, 0:r]).then_inc(at_copied, 1)
                s, g = j - 1, 1 - parity
                if valid(s):
                    r = rows(s)
                    act.wait_ge(tp_filled, s + 1)
                    at_least(act, lg_filled, s)
                    act.copy(t_t[:, :, 0:r], tp[:, :, 0:r]).then_inc(t_copied, 1)
                s, g = j, parity
                if valid(s):
                    r = rows(s)
                    act.wait_ge(h_done, s + 1)
                    at_least(act, t_done, s)
                    act.activation(unused[0:r, :], h[0:r, g, :], ACT.Square, scale=D ** -0.5,
                                   accum_out=mean[0:r, :]).then_inc(squared, 1)

            steps(act, body, 1, 3)

        @block.vector
        def _(dve):
            for k in range(DK):
                dve.wait_ge(piece_hi, k + 1)
                dve.tensor_tensor(w_lo[:, k, :], raw[:, k, :], w_hi[:, k, :].bitcast(F32), ALU.subtract)\
                    .then_inc(piece_lo, 1)
            dve.wait_ge(gain_loaded, 16)

            def body(j, parity):
                s, g = j - 2, parity
                if valid(s):
                    r = rows(s)
                    dve.wait_ge(lg_filled, s + 1)
                    if not (isinstance(s, int) and s == 0):
                        dve.wait_ge(aff_done, s)
                    dve.tensor_reduce(peak[0:r, :], lg[0:r, 0:E], AX_X, ALU.max, negate=True).then_inc(peak_done, 1)
                    dve.wait_ge(exp_done, s + 1)
                    dve.reciprocal(total[0:r, 1:2], total[0:r, 0:1]).then_inc(total_done, 1)
                    dve.wait_ge(total_done, s + 1)
                    dve.tensor_scalar(aff[0:r, :], aff[0:r, :], total[0:r, 1:2], None, ALU.mult).then_inc(aff_done, 1)
                s, g = j, parity
                if valid(s):
                    r = rows(s)
                    dve.wait_ge(acc_filled, s + 1)
                    if not isinstance(s, int) or s >= 2:
                        dve.wait_ge(stored[g], 32 * tile_index(s, g))
                        dve.wait_ge(tp_filled, s - 1)
                    dve.tensor_tensor(h[0:r, g, :], acc[0:r, g, :], x[0:r, g, :], ALU.add).then_inc(h_done, 1)
                    link = Chain(dve, chain, RSQRT_OPS, s)
                    dve.wait_ge(squared, s + 1)
                    rsqrt(dve, link, rs[0:r, 0, :], mean[0:r, :], rs[0:r, 1, :], rs[0:r, 2, :])
                    dve.scalar_tensor_tensor(t_tile[0:r, g, :], h[0:r, g, :], rs[0:r, 1, :], gain[0:r, :],
                                             ALU.mult, ALU.mult).then_inc(t_done, 1)
                    link.end()

            steps(dve, body, 1, 3)

        @block.gpsimd
        def _(pool):
            identity_matrix(pool, ident, ident_ready)



def choose(nc, io, scr, rows_t, gates_t, w_raw, w_hi, w_lo):
    LISTS = GROUPS * E
    ROUNDS = (CAP + 7) // 8
    with ExitStack() as ctx:
        def sb(name, shape, dt=F32):
            return ctx.enter_context(nc.sbuf_tensor("s_" + name, shape, dt))

        def sem(name):
            return nc.alloc_semaphore("s_" + name)

        aff = sb("aff", [LISTS, TOK])
        top, index = sb("top", [LISTS, ROUNDS * 8]), sb("index", [LISTS, ROUNDS * 8], U32)
        column, is_meta = sb("column", [LISTS, ROUNDS * 8]), sb("is_meta", [LISTS, ROUNDS * 8])
        row_map = sb("row_map", [LISTS, 2])
        ident = sb("ident", [P, P])
        tp = ctx.enter_context(nc.psum_tensor("s_tp", [P, 4, LISTS], F32))
        loaded, ident_ready, chain, ready, filled, done = (sem("loaded"), sem("ident_ready"), sem("chain"), sem("ready"),
                                                           sem("filled"), sem("done"))
        raw_loaded = [sem(f"raw_loaded{k}") for k in range(RAW)]
        slab_hi, slab_lo = sem("slab_hi"), sem("slab_lo")
        block = ctx.enter_context(nc.Block())

        @block.sync
        def _(sp):
            sp.dma_start(aff[:, :], scr["aff_t"][:, :]).then_inc(loaded, 16)
            sp.dma_start(row_map[:, :], io["row_map"]).then_inc(loaded, 16)
            for j in range(SLABS):
                at_least(sp, slab_lo, j - RAW + 1)
                load_slab(sp, io, w_raw, 0, j, raw_loaded)

        @block.scalar
        def _(act):
            for j in range(SLABS):
                act.wait_ge(raw_loaded[j % RAW], 32 * (j // RAW + 1))
                act.copy(w_hi[:, j, :], w_raw[:, j % RAW, :]).then_inc(slab_hi, 1)

        @block.vector
        def _(dve):
            dve.wait_ge(loaded, 32)
            link = Chain(dve, chain, 3 * ROUNDS + 2, 0)
            for i in range(ROUNDS):
                eight = slice(i * 8, i * 8 + 8)
                link(dve.max(top[:, eight], aff[:, :]))
                link(dve.max_index(index[:, eight], top[:, eight], aff[:, :]))
                link(dve.match_replace(aff[:, :], top[:, eight], aff[:, :], -1.0))
            link(dve.tensor_copy(column[:, :], index[:, :]))
            link(dve.tensor_scalar(is_meta[:, :], column[:, :], META - 0.5, row_map[:, 1:2], ALU.is_lt, ALU.mult))
            dve.scalar_tensor_tensor(column[:, :], column[:, :], row_map[:, 0:1], is_meta[:, :], ALU.add, ALU.add)\
                .then_inc(ready, 1)
            dve.wait_ge(filled, 1)
            dve.tensor_copy(rows_t[:, :, :], tp[0:HALF_CAP, 0:2, :]).then_inc(done, 1)
            dve.tensor_copy(gates_t[:, :, :], tp[0:HALF_CAP, 2:4, :]).then_inc(done, 1)

        @block.tensor
        def _(pe):
            pe.wait_ge(ident_ready, 2)
            pe.wait_ge(ready, 1)
            for k, tile in enumerate((column, top)):
                for half in range(2):
                    ins = pe.transpose(tp[0:HALF_CAP, 2 * k + half, :], tile[:, half * HALF_CAP:(half + 1) * HALF_CAP],
                                       ident[0:LISTS, 0:LISTS])
            ins.then_inc(filled, 1)

        @block.gpsimd
        def _(pool):
            identity_matrix(pool, ident, ident_ready)
            for j in range(SLABS):
                pool.wait_ge(slab_hi, j + 1)
                pool.tensor_tensor(w_lo[:, j, :], w_raw[:, j % RAW, :], w_hi[:, j, :].bitcast(F32), ALU.subtract)\
                    .then_inc(slab_lo, 1)


def experts(nc, io, scr, rows_t, gates_t, raw, w_hi, w_lo):
    NT = 2 * GROUPS
    W = NT * HALF_CAP
    LATE_SLABS = {1: 3, 5: 4, 7: 5}
    with ExitStack() as ctx:
        def sb(name, shape, dt=F32):
            return ctx.enter_context(nc.sbuf_tensor("e_" + name, shape, dt))

        def sem(name):
            return nc.alloc_semaphore("e_" + name)

        rows_now = sb("rows_now", [HALF_CAP, 2, GROUPS], U32)
        gathered = sb("gathered", [HALF_CAP, NT, D])
        x_hi, x_lo = sb("x_hi", [P, DK, W], F32R), sb("x_lo", [P, DK, W], F32R)
        silu = sb("silu", [P, 2, W])
        act_h = sb("act_h", [P, 2, W])
        h_hi, h_lo = sb("h_hi", [P, FK, W], F32R), sb("h_lo", [P, FK, W], F32R)
        y_t = sb("y_t", [P, DK, W])
        y = sb("y", [HALF_CAP, NT, D])
        rows_out = sb("rows_out", [HALF_CAP, 2, GROUPS], U32)
        ident = sb("ident", [P, P])
        gu = ctx.enter_context(nc.psum_tensor("e_gu", [P, 2, 2, 512], F32))
        tp = ctx.enter_context(nc.psum_tensor("e_tp", [P, 2, 512], F32))
        dn = ctx.enter_context(nc.psum_tensor("e_dn", [P, 2, 512], F32))

        raw_loaded = [sem(f"raw_loaded{k}") for k in range(RAW)]
        slab_hi, slab_lo, ident_ready, sp_passed = sem("slab_hi"), sem("slab_lo"), sem("ident_ready"), sem("sp_passed")
        rows_copied, gathered_sem, x_filled, x_hi_done, x_lo_done = (
            sem("rows_copied"), sem("gathered"), sem("x_filled"), sem("x_hi_done"), sem("x_lo_done"))
        gu_filled, silu_done, h_done, h_hi_done, h_lo_done = (
            sem("gu_filled"), sem("silu_done"), sem("h_done"), sem("h_hi_done"), sem("h_lo_done"))
        dn_filled, y_t_act, y_t_dve, y_filled, y_act, y_dve = (
            sem("dn_filled"), sem("y_t_act"), sem("y_t_dve"), sem("y_filled"), sem("y_act"), sem("y_dve"))
        scattered, pool_passed, out_rows_copied = sem("scattered"), sem("pool_passed"), sem("out_rows_copied")
        gates_now, gates_copied = sb("gates_now", [HALF_CAP, 2, GROUPS]), sem("gates_copied")
        block = ctx.enter_context(nc.Block())

        def columns(tile, e):
            return tile[:, :, :].rearrange("p h (g e) -> p h g e", g=GROUPS)[:, :, :, bass.ds(e, 1)]\
                .rearrange("p h g o -> p h (g o)")

        def slab_number(e, j):
            return SLABS * (e - 1) + j

        def each_expert(eng, body):
            body(0)
            with eng.Fori(1, E - 1) as e:
                body(e)
            body(E - 1)

        def is_first(e):
            return isinstance(e, int) and e == 0

        def is_last(e):
            return isinstance(e, int) and e == E - 1

        @block.sync
        def _(sp):
            def body(e):
                for j in range(SLABS):
                    wait_alone(sp, slab_lo, slab_number(e, j) - RAW + 1, sp_passed)
                    load_slab(sp, io, raw, e, j, raw_loaded)

            body(1)
            with sp.Fori(2, E) as e:
                body(e)

        @block.tensor
        def _(pe):
            pe.wait_ge(ident_ready, 2)

            def tokens_of(e, k):
                if k == 0:
                    pe.wait_ge(gathered_sem, 16 * NT * (e + 1))
                n = DK * e + k
                at_least(pe, x_hi_done, n - 1)
                at_least(pe, x_lo_done, n - 1)
                if k < 2:
                    at_least(pe, y_act, NT * (e - 1))
                    at_least(pe, y_dve, NT * (e - 1))
                for t in range(NT):
                    ins = pe.transpose(tp[:, k % 2, t * HALF_CAP:(t + 1) * HALF_CAP],
                                       gathered[:, t, k * P:(k + 1) * P], ident[0:HALF_CAP, 0:HALF_CAP])
                ins.then_inc(x_filled, 1)

            def gate_up(e):
                pe.wait_ge(x_lo_done, DK * (e + 1))
                for j in range(FK):
                    n = FK * e + j
                    if not is_first(e):
                        pe.wait_ge(slab_lo, slab_number(e, j) + 1)
                    at_least(pe, h_done, n - 1)
                    for a in range(2):
                        for k in range(DK):
                            at = (a * DK + k) * P
                            for q, (w, t) in enumerate(((w_hi, x_hi), (w_hi, x_lo), (w_lo, x_hi))):
                                ins = pe.matmul(gu[:, j % 2, a, 0:W], w[:, j, at:at + P], t[:, k, :],
                                                start=(k == 0 and q == 0), stop=(k == DK - 1 and q == 2))
                    ins.then_inc(gu_filled, 1)
                    if not is_first(e):
                        results_of(e - 1, j)

            def down(e):
                def column_tile(m, parts):
                    for k in parts:
                        at = k * 512 + (m % 4) * P
                        for q, (w, t) in enumerate(((w_hi, h_hi), (w_hi, h_lo), (w_lo, h_hi))):
                            ins = pe.matmul(dn[:, m % 2, 0:W], w[:, FK + m // 4, at:at + P], t[:, k, :],
                                            start=(k == 0 and q == 0), stop=(k == FK - 1 and q == 2))
                    return ins

                def bank_free(m):
                    at_least(pe, y_t_act if m % 2 == 0 else y_t_dve, DK // 2 * e + m // 2)

                pe.wait_ge(h_lo_done, FK * (e + 1) - 1)
                if not is_first(e):
                    pe.wait_ge(slab_lo, slab_number(e, FK) + 1)
                for m in range(2):
                    bank_free(m)
                    column_tile(m, range(FK - 1))
                if not is_last(e):
                    tokens_of(e + 1, 0)
                    tokens_of(e + 1, 1)
                pe.wait_ge(h_lo_done, FK * (e + 1))
                for m in range(DK):
                    if m == 4 and not is_first(e):
                        pe.wait_ge(slab_lo, slab_number(e, FK + 1) + 1)
                    if m >= 2:
                        bank_free(m)
                    column_tile(m, range(FK - 1 if m < 2 else 0, FK)).then_inc(dn_filled, 1)
                    if not is_last(e) and m + 2 < DK:
                        tokens_of(e + 1, m + 2)

            def results_of(e, t):
                if t == 0:
                    pe.wait_ge(y_t_act, DK // 2 * (e + 1))
                    pe.wait_ge(y_t_dve, DK // 2 * (e + 1))
                    at = e + 2 if not is_last(e) else e + 1
                    pe.wait_ge(x_hi_done, DK * at)
                    pe.wait_ge(x_lo_done, DK * at)
                for half in range(2):
                    at_least(pe, y_act if half == 0 else y_dve, NT * e + t)
                    for k in range(4):
                        ins = pe.transpose(tp[0:HALF_CAP, half, k * P:(k + 1) * P],
                                           y_t[:, half * 4 + k, t * HALF_CAP:(t + 1) * HALF_CAP], ident[:, :])
                    ins.then_inc(y_filled, 1)

            for k in range(DK):
                tokens_of(0, k)

            def body(e):
                gate_up(e)
                down(e)

            each_expert(pe, body)
            for t in range(NT):
                results_of(E - 1, t)

        @block.scalar
        def _(act):
            def slab(e, j):
                act.wait_ge(raw_loaded[j % RAW], 32 * (2 * (e - 1) + j // RAW + 1))
                if j < FK:
                    act.wait_ge(gu_filled, FK * (e - 1) + j + 1)
                else:
                    act.wait_ge(dn_filled, DK * (e - 1) + 4 * (j - FK + 1))
                act.copy(w_hi[:, j, :], raw[:, j % RAW, :]).then_inc(slab_hi, 1)

            def tokens(e, k):
                act.wait_ge(x_filled, DK * e + k + 1)
                if k == 0:
                    at_least(act, gu_filled, FK * e)
                act.copy(x_hi[:, k, :], tp[:, k % 2, 0:W]).then_inc(x_hi_done, 1)

            def hidden(e, j):
                n = FK * e + j
                act.wait_ge(gu_filled, n + 1)
                at_least(act, h_done, n - 1)
                act.activation(silu[:, j % 2, :], gu[:, j % 2, 0, 0:W], ACT.Silu).then_inc(silu_done, 1)
                act.wait_ge(h_done, n + 1)
                if j == 0:
                    at_least(act, dn_filled, DK * e)
                act.copy(h_hi[:, j, :], act_h[:, j % 2, :]).then_inc(h_hi_done, 1)

            def transposed(e, m):
                act.wait_ge(dn_filled, DK * e + m + 1)
                at_least(act, y_filled, 2 * NT * e)
                act.copy(y_t[:, m, :], dn[:, m % 2, 0:W]).then_inc(y_t_act, 1)

            def results(e, t):
                act.wait_ge(y_filled, 2 * (NT * e + t) + 1)
                at_least(act, scattered, 16 * NT * e)
                act.wait_ge(gates_copied, e + 1)
                act.activation(y[:, t, 0:512], tp[0:HALF_CAP, 0, :], ACT.Copy, scale=gates_now[:, t % 2, t // 2:t // 2 + 1])\
                    .then_inc(y_act, 1)

            for k in range(DK):
                tokens(0, k)

            def body(e):
                for j in range(FK):
                    hidden(e, j)
                    if not is_first(e):
                        results(e - 1, j)
                    if not is_last(e) and j < 3:
                        slab(e + 1, j)
                if not is_last(e):
                    tokens(e + 1, 0)
                    tokens(e + 1, 1)
                for m in range(DK):
                    if m % 2 == 0:
                        transposed(e, m)
                    if not is_last(e) and m + 2 < DK:
                        tokens(e + 1, m + 2)
                    if not is_last(e) and m in LATE_SLABS:
                        slab(e + 1, LATE_SLABS[m])

            each_expert(act, body)
            for t in range(NT):
                results(E - 1, t)

        @block.vector
        def _(dve):
            def slab(e, j):
                dve.wait_ge(slab_hi, slab_number(e, j) + 1)
                dve.tensor_tensor(w_lo[:, j, :], raw[:, j % RAW, :], w_hi[:, j, :].bitcast(F32), ALU.subtract)\
                    .then_inc(slab_lo, 1)

            def tokens(e, k):
                dve.wait_ge(x_hi_done, DK * e + k + 1)
                dve.tensor_tensor(x_lo[:, k, :], tp[:, k % 2, 0:W], x_hi[:, k, :].bitcast(F32), ALU.subtract)\
                    .then_inc(x_lo_done, 1)

            def hidden(e, j):
                n = FK * e + j
                dve.wait_ge(silu_done, n + 1)
                at_least(dve, h_hi_done, n - 1)
                dve.tensor_tensor(act_h[:, j % 2, :], gu[:, j % 2, 1, 0:W], silu[:, j % 2, :], ALU.mult)\
                    .then_inc(h_done, 1)
                dve.wait_ge(h_hi_done, n + 1)
                dve.tensor_tensor(h_lo[:, j, :], act_h[:, j % 2, :], h_hi[:, j, :].bitcast(F32), ALU.subtract)\
                    .then_inc(h_lo_done, 1)

            def transposed(e, m):
                dve.wait_ge(dn_filled, DK * e + m + 1)
                at_least(dve, y_filled, 2 * NT * e)
                dve.tensor_copy(y_t[:, m, :], dn[:, m % 2, 0:W]).then_inc(y_t_dve, 1)

            def results(e, t):
                dve.wait_ge(y_filled, 2 * (NT * e + t) + 2)
                at_least(dve, scattered, 16 * NT * e)
                dve.tensor_scalar(y[:, t, 512:D], tp[0:HALF_CAP, 1, :], gates_now[:, t % 2, t // 2:t // 2 + 1], None,
                                  ALU.mult).then_inc(y_dve, 1)

            for k in range(DK):
                tokens(0, k)

            def gates_of(e):
                at_least(dve, y_act, NT * e)
                at_least(dve, y_dve, NT * e)
                dve.tensor_copy(gates_now[:, :, :], columns(gates_t, e)).then_inc(gates_copied, 1)
                dve.wait_ge(gates_copied, e + 1)

            def body(e):
                if not is_first(e):
                    gates_of(e - 1)
                for j in range(FK):
                    hidden(e, j)
                    if not is_first(e):
                        results(e - 1, j)
                    if not is_last(e) and j < 3:
                        slab(e + 1, j)
                if not is_last(e):
                    tokens(e + 1, 0)
                    tokens(e + 1, 1)
                for m in range(DK):
                    if m % 2 == 1:
                        transposed(e, m)
                    if not is_last(e) and m + 2 < DK:
                        tokens(e + 1, m + 2)
                    if not is_last(e) and m in LATE_SLABS:
                        slab(e + 1, LATE_SLABS[m])

            each_expert(dve, body)
            gates_of(E - 1)
            for t in range(NT):
                results(E - 1, t)

        @block.gpsimd
        def _(pool):
            identity_matrix(pool, ident, ident_ready)

            def gather(e):
                if not is_first(e):
                    wait_alone(pool, x_filled, DK * e, pool_passed)
                    wait_alone(pool, gathered_sem, 16 * NT * e, pool_passed)
                pool.tensor_copy(rows_now[:, :, :], columns(rows_t, e)).then_inc(rows_copied, 1)
                wait_alone(pool, rows_copied, e + 1, pool_passed)
                for t in range(NT):
                    pool.indirect_dma_start(
                        out=gathered[:, t, :], out_offset=None, in_=scr["t_rows"][:, :],
                        in_offset=bass.IndirectOffsetOnAxis(ap=rows_now[:, t % 2, t // 2:t // 2 + 1], axis=0))\
                        .then_inc(gathered_sem, 16)

            def scatter(e):
                if not is_first(e):
                    wait_alone(pool, scattered, 16 * NT * e, pool_passed)
                pool.tensor_copy(rows_out[:, :, :], columns(rows_t, e)).then_inc(out_rows_copied, 1)
                wait_alone(pool, y_act, NT * (e + 1), pool_passed)
                wait_alone(pool, y_dve, NT * (e + 1), pool_passed)
                wait_alone(pool, out_rows_copied, e + 1, pool_passed)
                for t in range(NT):
                    pool.indirect_dma_start(
                        out=scr["h_rows"][:, :],
                        out_offset=bass.IndirectOffsetOnAxis(ap=rows_out[:, t % 2, t // 2:t // 2 + 1], axis=0),
                        in_=y[:, t, :], in_offset=None, compute_op=ALU.add).then_inc(scattered, 16)

            gather(0)

            def body(e):
                if not is_last(e):
                    gather(e + 1)
                if not is_first(e):
                    scatter(e - 1)

            each_expert(pool, body)
            scatter(E - 1)
            pool.wait_ge(scattered, 16 * NT * E)


def finish(nc, io, scr, outs):
    with ExitStack() as ctx:
        def sb(name, shape, dt=F32):
            return ctx.enter_context(nc.sbuf_tensor("f_" + name, shape, dt))

        def sem(name):
            return nc.alloc_semaphore("f_" + name)

        N = GROUPS * XCH
        DEEP = 4
        h, y = sb("h", [P, DEEP, D]), sb("y", [P, DEEP, D])
        unused, gain = sb("unused", [P, D]), sb("gain", [P, D])
        mean, rs = sb("mean", [P, 2]), sb("rs", [P, 3, 1])
        gain_loaded, squared, chain, done = sem("gain_loaded"), sem("squared"), sem("chain"), sem("done")
        loaded, stored = [sem(f"loaded{k}") for k in range(DEEP)], [sem(f"stored{k}") for k in range(DEEP)]
        block = ctx.enter_context(nc.Block())

        @block.sync
        def _(sp):
            sp.dma_start(gain[:, :], spread(io["final_norm"], 0, P)).then_inc(gain_loaded, 16)
            for n in range(N):
                at_least(sp, done, n - DEEP + 1)
                sp.dma_start(h[:, n % DEEP, :], scr["h_rows"][n * P:(n + 1) * P, :]).then_inc(loaded[n % DEEP], 16)

        def store(act, n):
            act.wait_ge(done, n + 1)
            act.dma_start(outs[n // XCH][0, (n % XCH) * P:(n % XCH + 1) * P, :], y[:, n % DEEP, :])\
                .then_inc(stored[n % DEEP], 16)

        @block.scalar
        def _(act):
            for n in range(N):
                act.wait_ge(loaded[n % DEEP], 16 * (n // DEEP + 1))
                at_least(act, done, n - 1)
                at_least(act, squared, n)
                act.activation(unused[:, :], h[:, n % DEEP, :], ACT.Square, scale=D ** -0.5,
                               accum_out=mean[:, n % 2:n % 2 + 1]).then_inc(squared, 1)
                if n > 0:
                    store(act, n - 1)
            store(act, N - 1)
            for k in range(DEEP):
                act.wait_ge(stored[k], 16 * (N // DEEP))

        @block.vector
        def _(dve):
            dve.wait_ge(gain_loaded, 16)
            for n in range(N):
                link = Chain(dve, chain, RSQRT_OPS, n)
                dve.wait_ge(squared, n + 1)
                rsqrt(dve, link, rs[:, 0, :], mean[:, n % 2:n % 2 + 1], rs[:, 1, :], rs[:, 2, :])
                if n >= DEEP:
                    dve.wait_ge(stored[n % DEEP], 16 * (n // DEEP))
                dve.scalar_tensor_tensor(y[:, n % DEEP, :], h[:, n % DEEP, :], rs[:, 1, :], gain[:, :],
                                         ALU.mult, ALU.mult).then_inc(done, 1)
                link.end()


def rope_table():
    import numpy as np
    grid = 64
    row = np.concatenate([np.repeat(np.arange(SEQ // grid), grid), np.full(META, -1)]).astype(np.float32)
    col = np.concatenate([np.tile(np.arange(grid), SEQ // grid), np.arange(META)]).astype(np.float32)
    parts = []
    for width in (HD, ROT):
        half = width // 4
        inv = np.float32(10000.0) ** (-np.arange(half, dtype=np.float32) / np.float32(half))
        cos, sin = [], []
        for pos in (row, col):
            angle = pos[:, None] * inv[None, :]
            c, s = np.cos(angle), np.sin(angle)
            cos += [c, c]
            sin += [-s, s]
        parts += cos + sin
    return np.ascontiguousarray(np.concatenate(parts, axis=1).astype(np.float32))


def row_map():
    import numpy as np
    g = np.repeat(np.arange(GROUPS), E)
    x_offset = SEQ * g - META
    meta_offset = GROUPS * SEQ + META * g
    return np.stack([x_offset, meta_offset - x_offset], axis=1).astype(np.float32)


def build(nc, io, outs):
    scr = scratch_tensors(nc)
    with nc.cleanup_on_exit():
        project(nc, io, scr)
        latents(nc, io, scr)
        attend(nc, io, scr, False)
        attend(nc, io, scr, True)
    mix(nc, io, scr)
    residual(nc, io, scr)
    with ExitStack() as ctx:
        rows_t = ctx.enter_context(nc.sbuf_tensor("rows_t", [HALF_CAP, 2, GROUPS * E], U32))
        gates_t = ctx.enter_context(nc.sbuf_tensor("gates_t", [HALF_CAP, 2, GROUPS * E], F32))
        w_raw = ctx.enter_context(nc.sbuf_tensor("w_raw", [P, RAW, SLAB], F32))
        w_hi = ctx.enter_context(nc.sbuf_tensor("w_hi", [P, SLABS, SLAB], F32R))
        w_lo = ctx.enter_context(nc.sbuf_tensor("w_lo", [P, SLABS, SLAB], F32R))
        choose(nc, io, scr, rows_t, gates_t, w_raw, w_hi, w_lo)
        experts(nc, io, scr, rows_t, gates_t, w_raw, w_hi, w_lo)
    finish(nc, io, scr, outs)


def kernel(**inputs):
    import numpy as _np
    import concourse.bacc as _bacc
    from concourse.bass_utils import run_bass_kernel_spmd as _run

    nc = _bacc.Bacc("TRN2", target_bir_lowering=False, num_devices=1)
    arrays = {name: _np.ascontiguousarray(a) for name, a in inputs.items()}
    arrays["rope"] = rope_table()
    arrays["row_map"] = row_map()
    io = {}
    for name, a in arrays.items():
        io[name] = nc.dram_tensor("in_" + name, a.shape, mybir.dt.from_np(a.dtype), kind="ExternalInput").ap()
    outs = [nc.dram_tensor(f"out_{g}", (1, SEQ, D), F32, kind="ExternalOutput").ap() for g in range(GROUPS)]
    build(nc, io, outs)
    r = _run(nc, [{"in_" + name: a for name, a in arrays.items()}], core_ids=[0])
    return tuple(r.results[0][f"out_{g}"] for g in range(GROUPS))
```
